# Optimizing a Trainium2 kernel written in Bass

```python
import math
import jax, jax.numpy as jnp
from jax import lax
import numpy as np

D_MODEL = 1024
BATCH = 1
SEQ = 512
DEPTH = 2
DEC_BATCH = 8
DEC_SEQ = 4
PAST_LEN = 2048
PAGE_SIZE = 128

N_META = 16
N_EVEN = (DEPTH + 1) // 2
N_ODD = DEPTH // 2
A_HEADS = 8
A_HEAD_DIM = D_MODEL // 16
A_KV_HEADS = 2
A_GROUP = A_HEADS // A_KV_HEADS
A_WIDTH = A_HEADS * A_HEAD_DIM
IDX_HEADS = 8
IDX_DIM = 64
TOPK_MAX = 256
Q_BLOCK = 128
POOL_WINDOWS = (2, 4, 8, 16)
POOL_GROUPS = 4
POOL_WIDTH = D_MODEL // 2
POOL_GROUP_DIM = POOL_WIDTH // POOL_GROUPS
POOL_BUF = 15
EVEN_SIZES = (A_WIDTH, A_KV_HEADS * A_HEAD_DIM, A_KV_HEADS * A_HEAD_DIM, IDX_HEADS * IDX_DIM, IDX_DIM, IDX_HEADS, POOL_WIDTH)
EVEN_IN = A_WIDTH + 2 * A_KV_HEADS * A_HEAD_DIM + IDX_HEADS * IDX_DIM + IDX_DIM + IDX_HEADS + POOL_WIDTH
EVEN_MIX = A_WIDTH + POOL_WIDTH
GLA_HEADS = 4
GLA_DK = D_MODEL // 2 // GLA_HEADS
GLA_DV = D_MODEL // GLA_HEADS
GLA_GATE_RANK = 16
GLA_GATE_NORM = 16.0
GLA_CHUNK = 64
ODD_SIZES = (GLA_HEADS * GLA_DK, GLA_HEADS * GLA_DK, GLA_HEADS * GLA_DV, GLA_HEADS * GLA_DV, GLA_GATE_RANK)
ODD_IN = 2 * GLA_HEADS * GLA_DK + 2 * GLA_HEADS * GLA_DV + GLA_GATE_RANK
ODD_MIX = GLA_HEADS * GLA_DV
D_FF = ((8 * D_MODEL + 3 * 256 - 1) // (3 * 256)) * 256
NORM_EPS = 1e-6

kernel_name = 'dsa_pool_gla_meta_hybrid_step'

def rmsnorm(x, g):
    xf = x.astype(jnp.float32)
    y = xf * lax.rsqrt(jnp.mean(xf * xf, axis=-1, keepdims=True) + NORM_EPS)
    return (y * g.astype(jnp.float32)).astype(x.dtype)

def split_cols(p, sizes):
    out, off = [], 0
    for s in sizes:
        out.append(p[..., off:off + s])
        off += s
    return out

def swiglu(h, wg, wu, wd):
    return (jax.nn.silu(h @ wg) * (h @ wu)) @ wd

def dsa_core(q, qi, wi, qpos, kidx, gather_kv, topk):
    B, T = q.shape[:2]
    Lk = kidx.shape[1]
    s = jnp.einsum('bthd,bsd->bths', qi.astype(jnp.float32), kidx.astype(jnp.float32))
    score = jnp.einsum('bths,bth->bts', jax.nn.relu(s), wi.astype(jnp.float32))
    vis = jnp.arange(Lk)[None, :] <= qpos[:, None]
    score = jnp.where(vis[None], score, -jnp.inf)
    _, idx = lax.top_k(score, topk)
    valid = idx <= qpos[None, :, None]
    k_sel, v_sel = gather_kv(idx)
    qg = q.reshape(B, T, A_KV_HEADS, A_GROUP, A_HEAD_DIM)
    logits = jnp.einsum('btkgd,btjkd->btkgj', qg, k_sel).astype(jnp.float32) * (A_HEAD_DIM ** -0.5)
    logits = jnp.where(valid[:, :, None, None, :], logits, -jnp.inf)
    p = jax.nn.softmax(logits, axis=-1).astype(v_sel.dtype)
    o = jnp.einsum('btkgj,btjkd->btkgd', p, v_sel)
    return o.reshape(B, T, A_WIDTH)

def rows_gather(src, idx):
    return jax.vmap(lambda sb, ib: sb[ib])(src, idx)

def dsa_prompt(q, k, v, qi, ki, wi):
    B, L = q.shape[:2]
    topk = min(TOPK_MAX, L // 4)
    nb = -(-L // Q_BLOCK)
    Lpad = nb * Q_BLOCK
    pad = lambda t: jnp.pad(t, [(0, 0), (0, Lpad - L)] + [(0, 0)] * (t.ndim - 2))
    qp, qip, wip = pad(q), pad(qi), pad(wi)
    gather = lambda idx: (rows_gather(k, idx), rows_gather(v, idx))

    def block(start):
        sl = lambda t: lax.dynamic_slice_in_dim(t, start, Q_BLOCK, axis=1)
        qpos = start + jnp.arange(Q_BLOCK)
        return dsa_core(sl(qp), sl(qip), sl(wip), qpos, ki, gather, topk)

    out = lax.map(block, jnp.arange(nb) * Q_BLOCK)
    return jnp.moveaxis(out, 0, 1).reshape(B, Lpad, A_WIDTH)[:, :L]

def dsa_sample(q, k_new, v_new, qi, ki_new, wi, pool_k, pool_v, pool_ki, page_table):
    DB, T = q.shape[:2]
    past = page_table.shape[1] * PAGE_SIZE
    topk = min(TOPK_MAX, (past + T) // 4)
    ki_past = pool_ki[page_table].reshape(DB, past, IDX_DIM)
    ki_all = jnp.concatenate([ki_past.astype(ki_new.dtype), ki_new], axis=1)
    kflat = pool_k.reshape(-1, A_KV_HEADS, A_HEAD_DIM)
    vflat = pool_v.reshape(-1, A_KV_HEADS, A_HEAD_DIM)

    def gather(idx):
        ip = jnp.minimum(idx, past - 1)
        page = jax.vmap(lambda pt, i: pt[i])(page_table, ip // PAGE_SIZE)
        phys = page * PAGE_SIZE + ip % PAGE_SIZE
        inew = jnp.clip(idx - past, 0, T - 1)
        is_new = (idx >= past)[..., None, None]
        k_sel = jnp.where(is_new, rows_gather(k_new, inew), kflat[phys].astype(k_new.dtype))
        v_sel = jnp.where(is_new, rows_gather(v_new, inew), vflat[phys].astype(v_new.dtype))
        return k_sel, v_sel

    qpos = past + jnp.arange(T)
    return dsa_core(q, qi, wi, qpos, ki_all, gather, topk)

def multiscale_pool(u, prefix, pos, w_grp, scale):
    B, T, C = u.shape
    ext = jnp.concatenate([prefix, u], axis=1)
    extf = ext.astype(jnp.float32)
    cs = jnp.pad(jnp.cumsum(extf, axis=1), ((0, 0), (1, 0), (0, 0)))
    end = cs[:, POOL_BUF + 1:]
    outs = []
    for g, w in enumerate(POOL_WINDOWS):
        sl = slice(g * POOL_GROUP_DIM, (g + 1) * POOL_GROUP_DIM)
        start = cs[:, POOL_BUF + 1 - w:POOL_BUF + 1 - w + T, sl]
        cnt = jnp.minimum(w, pos + 1).astype(jnp.float32)[None, :, None]
        outs.append((end[..., sl] - start) / cnt - extf[:, POOL_BUF:, sl])
    d = jnp.stack(outs, axis=2).astype(u.dtype)
    y = jnp.einsum('btgc,gce->btge', d, w_grp).reshape(B, T, C)
    return y * scale, ext[:, -POOL_BUF:]

def even_project(h, w_in):
    B, T, _ = h.shape
    q, k, v, qi, ki, wi, u = split_cols(h @ w_in, EVEN_SIZES)
    return (q.reshape(B, T, A_HEADS, A_HEAD_DIM), k.reshape(B, T, A_KV_HEADS, A_HEAD_DIM),
            v.reshape(B, T, A_KV_HEADS, A_HEAD_DIM), qi.reshape(B, T, IDX_HEADS, IDX_DIM), ki, wi, u)

def even_prompt(h, w_in, w_out, pw, ps):
    B, L, _ = h.shape
    q, k, v, qi, ki, wi, u = even_project(h, w_in)
    oa = dsa_prompt(q, k, v, qi, ki, wi)
    prefix = jnp.zeros((B, POOL_BUF, POOL_WIDTH), u.dtype)
    ob, buf = multiscale_pool(u, prefix, jnp.arange(L), pw, ps)
    y = jnp.concatenate([oa.astype(h.dtype), ob], axis=-1) @ w_out
    return y, k, v, ki, buf

def even_sample(h, pool_k, pool_v, pool_ki, buf0, page_table, w_in, w_out, pw, ps):
    T = h.shape[1]
    q, k, v, qi, ki, wi, u = even_project(h, w_in)
    past = page_table.shape[1] * PAGE_SIZE
    oa = dsa_sample(q, k, v, qi, ki, wi, pool_k, pool_v, pool_ki, page_table)
    ob, buf = multiscale_pool(u, buf0.astype(u.dtype), past + jnp.arange(T), pw, ps)
    y = jnp.concatenate([oa.astype(h.dtype), ob], axis=-1) @ w_out
    return y, k, v, ki, buf

def gla_scan(q, k, v, loga, S, chunk):
    B, T, H, DK = q.shape
    DV = v.shape[-1]
    n = T // chunk
    to_chunks = lambda t: jnp.moveaxis(t.astype(jnp.float32).reshape(B, n, chunk, H, t.shape[-1]), 1, 0)
    causal = jnp.tril(jnp.ones((chunk, chunk), bool))[None, :, :, None, None]

    def step(S, xs):
        qc, kc, vc, gc = xs
        b = jnp.cumsum(gc, axis=1)
        o_inter = jnp.einsum('bthd,bhde->bthe', qc * jnp.exp(b), S)
        diff = b[:, :, None] - b[:, None, :]
        decay = jnp.exp(jnp.where(causal, diff, -jnp.inf))
        att = jnp.einsum('bthd,bshd,btshd->bths', qc, kc, decay)
        o_intra = jnp.einsum('bths,bshe->bthe', att, vc)
        bl = b[:, -1]
        S = jnp.exp(bl)[..., None] * S + jnp.einsum('bshd,bshe->bhde', kc * jnp.exp(bl[:, None] - b), vc)
        return S, o_inter + o_intra

    S, o = lax.scan(step, S.astype(jnp.float32), (to_chunks(q), to_chunks(k), to_chunks(v), to_chunks(loga)))
    return jnp.moveaxis(o, 0, 1).reshape(B, T, H, DV), S

def gla_project(h, w_in, wgu, bg):
    B, T, _ = h.shape
    q, k, v, g, gd = split_cols(h @ w_in, ODD_SIZES)
    q = q.reshape(B, T, GLA_HEADS, GLA_DK) * (GLA_DK ** -0.5)
    k = k.reshape(B, T, GLA_HEADS, GLA_DK)
    v = v.reshape(B, T, GLA_HEADS, GLA_DV)
    loga = jax.nn.log_sigmoid((gd @ wgu + bg).astype(jnp.float32)) / GLA_GATE_NORM
    return q, k, v, g, loga.reshape(B, T, GLA_HEADS, GLA_DK)

def gla_output(o, g, gn, w_out, dtype):
    B, T = o.shape[:2]
    on = rmsnorm(o, gn).astype(dtype)
    on = on * jax.nn.silu(g.reshape(B, T, GLA_HEADS, GLA_DV))
    return on.reshape(B, T, ODD_MIX) @ w_out

def odd_prompt(h, w_in, wgu, bg, gn, w_out):
    B, L, _ = h.shape
    q, k, v, g, la = gla_project(h, w_in, wgu, bg)
    S0 = jnp.zeros((B, GLA_HEADS, GLA_DK, GLA_DV), jnp.float32)
    head = lambda t: t[:, :N_META]
    tail = lambda t: t[:, N_META:]
    o_m, S = gla_scan(head(q), head(k), head(v), head(la), S0, N_META)
    o_r, S = gla_scan(tail(q), tail(k), tail(v), tail(la), S, math.gcd(GLA_CHUNK, L - N_META))
    o = jnp.concatenate([o_m, o_r], axis=1)
    return gla_output(o, g, gn, w_out, h.dtype), S.astype(h.dtype)

def odd_sample(h, S0, w_in, wgu, bg, gn, w_out):
    T = h.shape[1]
    q, k, v, g, la = gla_project(h, w_in, wgu, bg)
    o, S = gla_scan(q, k, v, la, S0, math.gcd(GLA_CHUNK, T))
    return gla_output(o, g, gn, w_out, h.dtype), S.astype(h.dtype)

def setup_inputs(seed: int = 0) -> dict:
    key = jax.random.key(seed)
    ks = jax.random.split(key, 26)
    nrm = lambda k, shape, s: jax.random.normal(k, shape, jnp.float32) * s
    n_pages = PAST_LEN // PAGE_SIZE
    n_used = DEC_BATCH * n_pages
    n_pool = n_used + max(1, n_used // 4)
    page_table = jax.random.permutation(ks[0], n_pool)[:n_used].reshape(DEC_BATCH, n_pages).astype(jnp.int32)
    out_s = (2 * DEPTH) ** -0.5
    return {
        'x_prompt': nrm(ks[1], (BATCH, SEQ, D_MODEL), 1.0),
        'x_sample': nrm(ks[2], (DEC_BATCH, DEC_SEQ, D_MODEL), 1.0),
        'cache_k': nrm(ks[3], (N_EVEN, n_pool, PAGE_SIZE, A_KV_HEADS, A_HEAD_DIM), 1.0),
        'cache_v': nrm(ks[4], (N_EVEN, n_pool, PAGE_SIZE, A_KV_HEADS, A_HEAD_DIM), 1.0),
        'cache_kidx': nrm(ks[5], (N_EVEN, n_pool, PAGE_SIZE, IDX_DIM), 1.0),
        'state_pool': nrm(ks[6], (N_EVEN, DEC_BATCH, POOL_BUF, POOL_WIDTH), 1.0),
        'state_gla': nrm(ks[7], (N_ODD, DEC_BATCH, GLA_HEADS, GLA_DK, GLA_DV), 1.0),
        'page_table': page_table,
        'meta_tokens': nrm(ks[8], (N_META, D_MODEL), 1.0),
        'norm_mix': 1.0 + nrm(ks[9], (DEPTH, D_MODEL), 0.05),
        'norm_ffn': 1.0 + nrm(ks[10], (DEPTH, D_MODEL), 0.05),
        'norm_final': 1.0 + nrm(ks[11], (D_MODEL,), 0.05),
        'w_in_even': nrm(ks[12], (N_EVEN, D_MODEL, EVEN_IN), D_MODEL ** -0.5),
        'w_out_even': nrm(ks[13], (N_EVEN, EVEN_MIX, D_MODEL), EVEN_MIX ** -0.5 * out_s),
        'pool_w': nrm(ks[14], (N_EVEN, POOL_GROUPS, POOL_GROUP_DIM, POOL_GROUP_DIM), POOL_GROUP_DIM ** -0.5),
        'pool_scale': 1.0 + nrm(ks[15], (N_EVEN, POOL_WIDTH), 0.1),
        'w_in_odd': nrm(ks[16], (N_ODD, D_MODEL, ODD_IN), D_MODEL ** -0.5),
        'gla_w_gate_up': nrm(ks[17], (N_ODD, GLA_GATE_RANK, GLA_HEADS * GLA_DK), GLA_GATE_RANK ** -0.5),
        'gla_b_gate': nrm(ks[18], (N_ODD, GLA_HEADS * GLA_DK), 0.1),
        'gla_norm': 1.0 + nrm(ks[19], (N_ODD, GLA_DV), 0.05),
        'w_out_odd': nrm(ks[20], (N_ODD, ODD_MIX, D_MODEL), ODD_MIX ** -0.5 * out_s),
        'ffn_w_gate': nrm(ks[21], (DEPTH, D_MODEL, D_FF), D_MODEL ** -0.5),
        'ffn_w_up': nrm(ks[22], (DEPTH, D_MODEL, D_FF), D_MODEL ** -0.5),
        'ffn_w_down': nrm(ks[23], (DEPTH, D_FF, D_MODEL), D_FF ** -0.5 * out_s),
    }

def reference(x_prompt, x_sample, cache_k, cache_v, cache_kidx, state_pool, state_gla, page_table,
              meta_tokens, norm_mix, norm_ffn, norm_final, w_in_even, w_out_even, pool_w, pool_scale,
              w_in_odd, gla_w_gate_up, gla_b_gate, gla_norm, w_out_odd, ffn_w_gate, ffn_w_up, ffn_w_down):
    B = x_prompt.shape[0]
    meta = jnp.broadcast_to(meta_tokens.astype(x_prompt.dtype)[None], (B, N_META, D_MODEL))
    xp = jnp.concatenate([meta, x_prompt], axis=1)
    xs = x_sample
    kp_l, vp_l, kip_l, bp_l, ks_l, vs_l, kis_l, bs_l, Sp_l, Ss_l = [], [], [], [], [], [], [], [], [], []
    for l in range(DEPTH):
        hp = rmsnorm(xp, norm_mix[l])
        hs = rmsnorm(xs, norm_mix[l])
        if l % 2 == 0:
            e = l // 2
            yp, kp, vp, kip, bp = even_prompt(hp, w_in_even[e], w_out_even[e], pool_w[e], pool_scale[e])
            ys, kss, vss, kis, bs = even_sample(hs, cache_k[e], cache_v[e], cache_kidx[e], state_pool[e], page_table,
                                                w_in_even[e], w_out_even[e], pool_w[e], pool_scale[e])
            kp_l.append(kp); vp_l.append(vp); kip_l.append(kip); bp_l.append(bp)
            ks_l.append(kss); vs_l.append(vss); kis_l.append(kis); bs_l.append(bs)
        else:
            o = l // 2
            yp, Sp = odd_prompt(hp, w_in_odd[o], gla_w_gate_up[o], gla_b_gate[o], gla_norm[o], w_out_odd[o])
            ys, Ss = odd_sample(hs, state_gla[o], w_in_odd[o], gla_w_gate_up[o], gla_b_gate[o], gla_norm[o], w_out_odd[o])
            Sp_l.append(Sp); Ss_l.append(Ss)
        xp = xp + yp
        xs = xs + ys
        xp = xp + swiglu(rmsnorm(xp, norm_ffn[l]), ffn_w_gate[l], ffn_w_up[l], ffn_w_down[l])
        xs = xs + swiglu(rmsnorm(xs, norm_ffn[l]), ffn_w_gate[l], ffn_w_up[l], ffn_w_down[l])
    y_prompt = rmsnorm(xp, norm_final)[:, N_META:]
    y_sample = rmsnorm(xs, norm_final)
    return (y_prompt, y_sample,
            jnp.stack(kp_l), jnp.stack(vp_l), jnp.stack(kip_l),
            jnp.stack(ks_l), jnp.stack(vs_l), jnp.stack(kis_l),
            jnp.stack(bp_l), jnp.stack(bs_l),
            jnp.stack(Sp_l), jnp.stack(Ss_l))


_drawn_inputs = setup_inputs


def setup_inputs(seed=0):
    import zlib

    import numpy as np

    out = dict(_drawn_inputs(seed))
    spreads = {}
    factors = {'gla_norm': 4.21}
    for name, (base, spread) in spreads.items():
        noise = np.random.default_rng([zlib.crc32(name.encode()), seed]).standard_normal(out[name].shape)
        drawn = base * np.exp(spread * noise) if base else spread * noise
        out[name] = __import__('jax').numpy.asarray(drawn.astype(out[name].dtype))
    for name, factor in factors.items():
        out[name] = (out[name] * factor).astype(out[name].dtype)
    return out
```

```python
from contextlib import ExitStack

import concourse.bass as bass
from concourse import mybir

ALU = mybir.AluOpType
ACT = mybir.ActivationFunctionType
F32 = mybir.dt.float32
F32R = mybir.dt.float32r
BF16 = mybir.dt.bfloat16
I32 = mybir.dt.int32
AX = mybir.AxisListType
ds = bass.ds

P = 128
D = 1024
KC = D // P
META = 16
SEQ = 512
LP = META + SEQ
DB, DT = 8, 4
NS = DB * DT
R = LP + NS
HALF = R // 2
RB = 112
NRB = R // RB
LAST = LP - (NRB - 1) * RB
EPS = 1e-6

HD = 64
NH, NKV, GRP = 8, 2, 4
IH = 8
PAST, PAGE = 2048, 128
TOK = 16
SUB = PAGE // TOK
NPG = PAST // PAGE
SKEYS = PAST + NS
TOPK_P = min(256, LP // 4)
TOPK_S = min(256, (PAST + DT) // 4)
PADS = -TOPK_P % 8
ROUNDS_P = (TOPK_P + PADS) // 8
ROUNDS_S = TOPK_S // 8
PAD_SCORE, HIDDEN, TAKEN, TAKEN_CUT = 3.0e38, -1.0e38, -3.3e38, -3.2e38
NEG = -1.0e30
SCALE = HD ** -0.5

PB = 15
EXT = PB + LP
SEG = PB + DT
UEW = EXT + DB * SEG

FF = 2816
FT = FF // P
F_A, F_B = 12, 10

GH, GDK, GDV = 4, 128, 256
LEAD = 48
CH = 64
GW = LEAD + R
NCH = 10
GWP = NCH * CH
LEVELS = (64, 32, 16, 8, 4, 2)
GNORM = 16.0

C_ID, C_ONE, C_A8, C_DM, C_EX, C_VN, C_FN, C_INV = 0, 128, 256, 384, 448, 704, 736, 768
C_EPS, C_SUB = 832, 833
C_A = 834
G_ONE, G_MASK, G_RST, G_SB = 0, 128, 128 + 7 * 64, 128 + 7 * 64 + GWP
C_G = G_SB + DB

EVEN_SLABS = [(768, 256), (1024, 256), (512, 256), (1280, 72), (0, 256), (256, 256), (1352, 256), (1608, 256)]
EVEN_TILES = [2, 2, 2, 1, 2, 2, 2, 2]


class Count:

    def __init__(self, sem):
        self.sem, self.n = sem, 0

    def mark(self, ins):
        ins.then_inc(self.sem, 1)
        self.n += 1
        return self.n


class Gemm:

    def __init__(self, kind, slab0, use0, use1, iters, kcs=(KC, KC), **more):
        self.kind, self.slab0, self.use0, self.use1, self.iters, self.kcs = kind, slab0, use0, use1, iters, kcs
        self.done0 = use0 - (1 if use0 <= use1 + 1 else 2)
        self.slabs = 2 * iters
        self.more = more


def plan():
    out = {}
    s, u0, u1 = len(EVEN_SLABS), 8, 7

    def add(name, kind, iters, kcs=(KC, KC), uses=2, **more):
        nonlocal s, u0, u1
        g = Gemm(kind, s, u0, u1, iters, kcs, **more)
        out[name] = g
        s += 2 * iters
        u0 += uses * iters
        u1 += uses * iters

    def ffn(l):
        add(f"up{l}a", "up", 6, layer=l, f0=0)
        add(f"down{l}a", "down", 4, (6, 6), 1, layer=l, k0=0)
        add(f"up{l}b", "up", 5, layer=l, f0=F_A)
        add(f"down{l}b", "down", 4, (5, 5), 1, layer=l, k0=F_A)

    add("out0", "out", 2, layer=0)
    ffn(0)
    out["gd"] = Gemm("gd", s, u0, u1, 0)
    s += 1
    u0 += 1
    add("oq", "odd", 1, c0=0)
    add("okv", "odd", 3, c0=512)
    add("og", "odd", 2, c0=2048)
    add("out1", "out", 2, layer=1)
    ffn(1)
    return out, s


def trunk(nc, t, o):
    gemms, n_slabs = plan()
    norm_cols = {"mix0": 0, "mix1": 8, "ffn0": 16, "ffn1": 24, "final": 32}
    COL_PS, COL_BG, COL_GN = 40, 44, 48

    with ExitStack() as ctx:
        def sem(name):
            return ctx.enter_context(nc.semaphore(name))

        def sb(name, shape, dt):
            return ctx.enter_context(nc.sbuf_tensor(name, shape, dt))

        XT = sb("XT", [P, KC, R], F32)
        HHI = sb("HHI", [P, KC, R], F32R)
        HLO = sb("HLO", [P, KC, R], F32R)
        RAW = sb("RAW", [P, 2, KC, 256], F32)
        WHI = sb("WHI", [P, 2, KC, 256], F32R)
        WLO = sb("WLO", [P, 2, KC, 256], F32R)
        CA = sb("CA", [P, C_A], F32)
        COLS = sb("COLS", [P, 50], F32)
        IDB = sb("IDB", [P, P], BF16)
        EXB = sb("EXB", [NS, 2, P], BF16)
        NRM = sb("NRM", [P, 6, R], F32)
        base = nc.sbuf_base
        SQ, HT, RT, RR = NRM[:, 0:2, :], NRM[:, 2:4, :], NRM[:, 4, :], NRM[:, 5, :]
        PS = ctx.enter_context(nc.psum_tensor("PS", [P, 8, 512], F32))

        top = [0]

        def region(name, shape, dt, at=None):
            size = {F32: 4, F32R: 4, BF16: 2, I32: 4}[dt]
            n = size
            for x in shape[1:]:
                n *= x
            n = (n + 31) // 32 * 32
            if at is None:
                at = top[0]
                top[0] += n
            return nc.alloc_sbuf_tensor_at(name, shape, dt, offset=base + at), at, at + n

        KI, z_at, _ = region("KI", [P, 4, TOK, HD], F32)
        KIT, kit_at, _ = region("KIT", [P, 2, 1024], F32)
        XROW, _, _ = region("XROW", [RB, NRB, D], F32, z_at)
        KN, _, _ = region("KN", [P, 2, TOK, P], F32, z_at)
        KTS, _, _ = region("KTS", [P, PAST], F32, kit_at)
        SR, sr_at, _ = region("SR", [P, SKEYS], F32)
        PA, _, _ = region("PA", [P, 2, UEW], F32, sr_at)
        PD, _, _ = region("PD", [P, R], F32, sr_at + (2 * UEW * 4 + 31) // 32 * 32)
        QIT, qit_at, _ = region("QIT", [P, 4, R], F32, top[0])
        UE, _, ue_end = region("UE", [P, 4, UEW], F32, top[0])
        top[0] = ue_end
        SS, _, _ = region("SS", [NS, SKEYS], F32)
        NMS, _, _ = region("NMS", [NS, SKEYS], BF16)
        QT, _, _ = region("QT", [P, 4, R], F32)
        KT, _, _ = region("KT", [P, R], F32)
        KX, _, _ = region("KX", [P, R], F32)
        VT, _, _ = region("VT", [P, R], F32)
        KID, _, _ = region("KID", [P, R], F32)
        WIT, _, _ = region("WIT", [8, R], F32)
        KVR, _, _ = region("KVR", [RB, 6, 320], F32)
        SC, sc_at, _ = region("SC", [RB, 4, LP + PADS], F32, top[0])
        PTS, _, pts_end = region("PTS", [P, TOK + 1, P], F32, top[0])
        top[0] = pts_end
        NM, _, _ = region("NM", [RB, NRB, LP], BF16)
        QIS, _, _ = region("QIS", [P, DB, IH, DT], F32)
        WSEL, _, _ = region("WSEL", [P, 2, NS], F32)
        WIR, _, _ = region("WIR", [RB, NRB, IH], F32)
        M8, _, _ = region("M8", [RB, 4, 8], F32)
        M8S, _, _ = region("M8S", [NS, 8], F32)
        ST, _, _ = region("ST", [RB, 3, NRB * NH], F32)
        STS, _, _ = region("STS", [P, 8], F32)
        VEC, _, _ = region("VEC", [50, P], F32)
        SPN, _, _ = region("SPN", [DB * PB, 512], F32)
        PW, _, _ = region("PW", [P, 4, P], F32)
        PTB, _, _ = region("PTB", [P, DB], I32)
        PTF, _, _ = region("PTF", [P, DB], F32)
        PIX, _, _ = region("PIX", [P, DB], I32)
        QBD, _, _ = region("QBD", [P, DB, 2, GRP * DT], F32)
        UN, _, _ = region("UN", [P, 4, NS], F32)
        even_top = top[0]
        RL = nc.alloc_sbuf_tensor_at("RL", [RB, 2, LP], F32, offset=base - 6 * R * 4)
        PR = nc.alloc_sbuf_tensor_at("PR", [RB, 2, LP], F32, offset=base - 6 * R * 4)
        PT = nc.alloc_sbuf_tensor_at("PT", [RB, 2, NRB, RB], F32, offset=base - 6 * R * 4 + 2 * LP * 4)
        UO = nc.alloc_sbuf_tensor_at("UO", [NS, 2, 512], F32, offset=base - 6 * R * 4 + 2 * LP * 4 + 2 * NRB * RB * 4)

        top[0] = 0
        AHI, _, _ = region("AHI", [P, F_A, R], F32R)
        ALO, _, _ = region("ALO", [P, F_A, R], F32R)
        SG, _, _ = region("SG", [P, 2, R], F32)
        AT, _, _ = region("AT", [P, 2, R], F32)
        ffn_top = top[0]

        CG, _, _ = region("CG", [P, C_G], F32)
        WGU, _, _ = region("WGU", [16, GH * GDK], F32)
        GD, _, _ = region("GD", [16, R], F32)
        BC, _, odd_a = region("BC", [P, GH, GW], F32)
        top[0] = 0
        G, _, _ = region("G", [P, 16, GW], F32)
        ATT, _, _ = region("ATT", [P, 2, GW], F32)
        STATE, _, _ = region("STATE", [P, 2, GH, GDV], F32)
        LK, _, _ = region("LK", [P, 2, 2, GW], F32)
        assert top[0] <= ffn_top
        top[0] = odd_a
        EB, _, _ = region("EB", [P, GH, NCH - 1 + DB], F32)
        VR, _, _ = region("VR", [P, 2, 2 * GDV], F32)
        KR, _, _ = region("KR", [P, 2, 2 * GDK], F32)
        KB, shared, _ = region("KB", [96, 2, 2 * GDK], F32)
        shared = top[0]
        LQ, _, _ = region("LQ", [P, 2, 2, GW], F32)
        odd_top = top[0]
        top[0] = shared
        SIN, _, _ = region("SIN", [P, 2, GH, GDV], F32)
        SNEW, _, _ = region("SNEW", [P, 2, GH, GDV], F32)
        odd_top = max(odd_top, top[0])
        LE = NRM[:, :, :].rearrange("p a n -> p (a n)")[:, 0:4 * GW].rearrange("p (s h n) -> p s h n", s=2, h=2)
        GSC = NRM[:, 0:2, :]
        GRR = NRM[:, 2:6, :]
        YR, _, _ = region("YR", [RB, 4, 512], F32, 0)


        IDN = CA[:, C_ID:C_ID + P]
        ONE = CA[:, C_ONE:C_ONE + P]
        acc = [PS[:, 0:2, :], PS[:, 2:4, :]]

        def halves(a, n=P):
            return acc[a][0:n, :, 0:HALF]

        def halved(ap):
            return ap.rearrange("p (a n) -> p a n", a=2)

        in_consts, in_vecs, in_x, in_pt, in_spn, in_pw = (sem(n) for n in ("in_consts", "in_vecs", "in_x", "in_pt", "in_spn", "in_pw"))
        raw_in = [sem("raw_in0"), sem("raw_in1")]
        hi_done, lo_done, slab_used = sem("hi_done"), sem("lo_done"), sem("slab_used")
        acc_done, acc_free = sem("acc_done"), [sem("acc_free0"), sem("acc_free1")]
        vec_tr, cols_ready, x_tr, xe_d, xe_a = (sem(n) for n in ("vec_tr", "cols_ready", "x_tr", "xe_d", "xe_a"))
        sq_ready, sq_used, rt_ready, rr_ready, ht_ready, hhi_ready, h_ready = (
            sem(n) for n in ("sq_ready", "sq_used", "rt_ready", "rr_ready", "ht_ready", "hhi_ready", "h_ready"))
        casts, pix_ready = sem("casts"), sem("pix_ready")
        wi_tr, wir_ready, wsel_ready, qis_ready = (sem(n) for n in ("wi_tr", "wir_ready", "wsel_ready", "qis_ready"))
        il_ready, relu_done, sc_done, sc_masked, pads_set = (sem(n) for n in ("il_ready", "relu_done", "sc_done", "sc_masked", "pads_set"))
        kidx_in = [sem(f"kidx_in{i}") for i in range(4)]
        kit_tr, kit_ready, ss_done, sr_done, comb_done, comb_evac = (
            sem(n) for n in ("kit_tr", "kit_ready", "ss_done", "sr_done", "comb_done", "comb_evac"))
        tk, nm_ready, nm_final, tks, nms_ready, newscore = (sem(n) for n in ("tk", "nm_ready", "nm_final", "tks", "nms_ready", "newscore"))
        kvr_tr, kvr_ready, sp_tr, sp_ready, uo_tr, uo_ready = (sem(n) for n in ("kvr_tr", "kvr_ready", "sp_tr", "sp_ready", "uo_tr", "uo_ready"))
        u_zero, pool_step, pd_ready, y_done, yhi, ylo = (sem(n) for n in ("u_zero", "pool_step", "pd_ready", "y_done", "yhi", "ylo"))
        lg_ready, mx_ready, exp_done, rinv, pr_ready, pt_tr, pt_evac, pv_done, ohi, olo = (
            sem(n) for n in ("lg_ready", "mx_ready", "exp_done", "rinv", "pr_ready", "pt_tr", "pt_evac", "pv_done", "ohi", "olo"))
        kv_in = [sem("kv_in0"), sem("kv_in1")]
        qbd_ready, kts_tr, kts_evac, slg, smx, sexp, sstat, sp_norm, spt_tr, spt_evac, spv, sohi, solo = (
            sem(n) for n in ("qbd_ready", "kts_tr", "kts_evac", "slg", "smx", "sexp", "sstat", "sp_norm", "spt_tr", "spt_evac", "spv", "sohi", "solo"))
        ahi_ready, alo_ready = sem("ahi_ready"), sem("alo_ready")
        kts_evac2, spt_evac2, slg_mask = sem("kts_evac2"), sem("spt_evac2"), sem("slg_mask")
        out_done = sem("out_done")
        n_out = [0]

        in_cg, in_wgu, pads0, gd_ready = (sem(n) for n in ("in_cg", "in_wgu", "pads0", "gd_ready"))
        la_mm, la_abs, la_act, la_min, la_sub, b_ready = (sem(n) for n in ("la_mm", "la_abs", "la_act", "la_min", "la_sub", "b_ready"))
        lev_e, lev_x, lev_q, lev_k, att_done, att_ev, att_zero = (sem(n) for n in ("lev_e", "lev_x", "lev_q", "lev_k", "att_done", "att_ev", "att_zero"))
        kh_e, kh_x, qe_x, kh_ready, qe_ready, eb_ready = (sem(n) for n in ("kh_e", "kh_x", "qe_x", "kh_ready", "qe_ready", "eb_ready"))
        vk_tr, vk_ev, u_done, s_new, o_done, o_ev = (sem(n) for n in ("vk_tr", "vk_ev", "u_done", "s_new", "o_done", "o_ev"))
        st_in, st_out = [sem("st_in0"), sem("st_in1")], [sem("st_out0"), sem("st_out1")]
        kb_ready, oi_done, su_done, sn_ready, oi_ev = (sem(n) for n in ("kb_ready", "oi_done", "su_done", "sn_ready", "oi_ev"))
        osq_ready, osq_used, ort, orr, osc, gate_ready, o2hi, o2lo = (
            sem(n) for n in ("osq_ready", "osq_used", "ort", "orr", "osc", "gate_ready", "o2hi", "o2lo"))
        y_tr, yr_ready, yr_out = sem("y_tr"), sem("yr_ready"), [sem(f"yr_out{i}") for i in range(4)]

        def yr_total(slot, n):
            return sum(16 * (1 + (x % NRB == NRB - 1)) for x in range(n) if x % 4 == slot)

        NCP = NCH - 1
        WP = NCP * CH

        block = ctx.enter_context(nc.Block())

        a0, n_a = {}, 0
        for g in gemms.values():
            a0[g] = n_a
            n_a += 2 * g.iters if g.kind == "up" else 0

        def after(g, act_side=False):
            per = 1 if g.kind == "down" else 2
            return [(acc_free[0], g.use0 + per * g.iters), (acc_free[1], g.use1 + per * g.iters)]

        norms = [("mix0", [(xe_d, 5), (xe_a, 5)]), ("ffn0", after(gemms["out0"])), ("mix1", after(gemms["down0b"])),
                 ("ffn1", after(gemms["out1"])), ("final", after(gemms["down1b"]))]
        norm_no = {n: i for i, (n, _) in enumerate(norms)}

        def tile_done(g, a, n, slab):
            return (slab_used, g.slab0 + slab + 1) if a else (acc_done, g.done0 + n + 1)

        def blk(i):
            return (RB if i < NRB - 1 else LAST), min(RB * (i + 1), LP)

        def kv_order():
            return [(g, v, 4 * g + b) for g in range(2) for v in range(2) for b in range(4)]

        @block.sync
        def _(sp):
            sp.dma_start(CA[:, :], t["consts_a"]).then_inc(in_consts, 16)
            row = 0
            for name, n in (("norm_mix", 16), ("norm_ffn", 16), ("norm_final", 8), ("pool_scale", 4), ("gla_b_gate", 4), ("gla_norm", 2)):
                src = t[name]
                src = src.rearrange("(a n) -> a n", n=P) if len(src.shape) == 1 else src.rearrange("l (a n) -> (l a) n", n=P)
                sp.dma_start(VEC[row:row + n, :], src).then_inc(in_vecs, 16)
                row += n
            xp = t["x_prompt"][0]
            sp.dma_start(XROW[0:META, 0, :], t["meta_tokens"]).then_inc(in_x, 16)
            sp.dma_start(XROW[META:RB, 0, :], xp[0:RB - META, :]).then_inc(in_x, 16)
            lo = RB - META
            for i in range(1, 4):
                sp.dma_start(XROW[:, i, :], xp[lo:lo + RB, :]).then_inc(in_x, 16)
                lo += RB
            sp.dma_start(XROW[0:LAST, 4, :], xp[lo:SEQ, :]).then_inc(in_x, 16)
            sp.dma_start(XROW[LAST:RB, 4, :], t["x_sample"].rearrange("b t d -> (b t) d")).then_inc(in_x, 16)

            def load(s, src, kc, n):
                if s >= 2:
                    sp.wait_ge(lo_done, s - 1)
                sp.dma_start(RAW[:, s % 2, 0:kc, 0:n], src).then_inc(raw_in[s % 2], 16)

            w_even = t["w_in_even"][0].rearrange("(k p) n -> p k n", p=P)
            for s in range(4):
                c, n = EVEN_SLABS[s]
                load(s, w_even[:, :, c:c + n], KC, n)
            sp.dma_start(SPN[:, :], t["state_pool"][0].rearrange("b r c -> (b r) c")).then_inc(in_spn, 16)
            sp.dma_start(PW[:, :, :], t["pool_w"][0].rearrange("g c e -> c g e")).then_inc(in_pw, 16)
            for s in range(4, 6):
                c, n = EVEN_SLABS[s]
                load(s, w_even[:, :, c:c + n], KC, n)
            for s in range(6, 8):
                c, n = EVEN_SLABS[s]
                load(s, w_even[:, :, c:c + n], KC, n)

            def load_pair(g, i):
                a = g.slab0
                l = g.more.get("layer")
                if g.kind == "out":
                    w = t["w_out_even" if l == 0 else "w_out_odd"][0].rearrange("(k p) n -> p k n", p=P)
                    srcs = [w[:, :, ds(512 * i, 256)], w[:, :, ds(512 * i + 256, 256)]]
                elif g.kind == "up":
                    f0 = g.more["f0"] * P
                    srcs = [t[n][l].rearrange("(k p) n -> p k n", p=P)[:, :, ds(f0 + 256 * i, 256)] for n in ("ffn_w_gate", "ffn_w_up")]
                elif g.kind == "down":
                    w = t["ffn_w_down"][l].rearrange("(k p) n -> p k n", p=P)
                    k0, kc = g.more["k0"], g.kcs[0]
                    srcs = [w[:, k0:k0 + kc, ds(256 * i, 256)], w[:, k0 + kc:k0 + 2 * kc, ds(256 * i, 256)]]
                else:
                    w = t["w_in_odd"][0].rearrange("(k p) n -> p k n", p=P)
                    c0 = g.more["c0"]
                    srcs = [w[:, :, ds(c0 + 512 * i, 256)], w[:, :, ds(c0 + 512 * i + 256, 256)]]
                for j in range(2):
                    sp.wait_ge(lo_done, a + 2 * i + j - 1)
                    sp.dma_start(RAW[:, (a + j) % 2, 0:g.kcs[j], :], srcs[j]).then_inc(raw_in[(a + j) % 2], 16)

            def load_all(g):
                with sp.Fori(0, g.iters) as i:
                    load_pair(g, i)

            load_pair(gemms["out0"], 0)

            def store(dst, src):
                sp.dma_start(dst, src).then_inc(out_done, 16)
                n_out[0] += 1

            sp.wait_ge(kvr_ready, 6)
            for name, lo, n in (("k", 0, P), ("v", P, P), ("kidx", 2 * P, HD)):
                dst = o[f"new_{name}_prompt"]
                dst = dst[0, 0].rearrange("r h d -> r (h d)") if name != "kidx" else dst[0, 0]
                store(dst[0:4 * RB, :].rearrange("(i p) n -> p i n", p=RB), KVR[:, 0:4, lo:lo + n])
                store(dst[4 * RB:LP, :], KVR[0:LAST, 4, lo:lo + n])
                dst = o[f"new_{name}_sample"]
                dst = dst[0].rearrange("b t h d -> (b t) (h d)") if name != "kidx" else dst[0].rearrange("b t d -> (b t) d")
                store(dst, KVR[0:NS, 5, lo:lo + n])
            store(o["new_pool_sample"][0][:, 0:PB - DT, :], t["state_pool"][0][:, DT:PB, :])
            sp.wait_ge(uo_ready, 2)
            store(o["new_pool_prompt"][0, 0], UO[0:PB, 0, :])
            for b in range(DB):
                store(o["new_pool_sample"][0, b, PB - DT:PB, :], UO[DT * b:DT * b + DT, 1, :])

            load_pair(gemms["out0"], 1)
            for name in ("up0a", "down0a", "up0b", "down0b"):
                load_all(gemms[name])

            w_odd = t["w_in_odd"][0].rearrange("(k p) n -> p k n", p=P)
            sp.dma_start(CG[:, :], t["consts_g"]).then_inc(in_cg, 16)
            sp.dma_start(WGU[:, :], t["gla_w_gate_up"][0]).then_inc(in_wgu, 16)
            load(gemms["gd"].slab0, w_odd[:, :, 3072:3088], KC, 16)
            load_all(gemms["oq"])
            load_all(gemms["okv"])
            load_pair(gemms["og"], 0)
            sgla = t["state_gla"][0]
            for b in range(DB):
                if b == 0:
                    sp.wait_ge(qe_ready, 2)
                if b >= 2:
                    sp.wait_ge(sn_ready, GH * (b - 1))
                    sp.wait_ge(oi_done, b - 1)
                sp.dma_start(SIN[:, b % 2, :, :], sgla[b].rearrange("h d e -> d h e")).then_inc(st_in[b % 2], 16)
                if b:
                    sp.wait_ge(sn_ready, GH * b)
                    sp.dma_start(o["new_gla_sample"][0, b - 1].rearrange("h d e -> d h e"), SNEW[:, (b - 1) % 2, :, :]).then_inc(st_out[(b - 1) % 2], 16)
            sp.wait_ge(sn_ready, GH * DB)
            sp.dma_start(o["new_gla_sample"][0, DB - 1].rearrange("h d e -> d h e"), SNEW[:, 1, :, :]).then_inc(st_out[1], 16)
            sp.wait_ge(s_new, GH * NCP)
            store(o["new_gla_prompt"][0, 0].rearrange("h d e -> d h e"), STATE[:, NCP % 2, :, :])
            load_pair(gemms["og"], 1)
            for name in ("out1", "up1a", "down1a", "up1b", "down1b"):
                load_all(gemms[name])
            for n in range(2 * NRB):
                c4, i = divmod(n, NRB)
                sp.wait_ge(yr_ready, n + 1)
                cols = slice(512 * c4, 512 * c4 + 512)
                first = META if i == 0 else 0
                m = RB if i < NRB - 1 else LAST
                r0 = RB * i + first - META
                sp.dma_start(o["y_prompt"][0, r0:r0 + m - first, cols], YR[first:m, n % 4, :]).then_inc(yr_out[n % 4], 16)
                if i == NRB - 1:
                    sp.dma_start(o["y_sample"].rearrange("b t d -> (b t) d")[:, cols], YR[LAST:RB, n % 4, :]).then_inc(yr_out[n % 4], 16)
            for n in range(4):
                sp.wait_ge(yr_out[n], yr_total(n, 2 * NRB))
            for n in range(2):
                sp.wait_ge(st_out[n], 16 * DB // 2)
            sp.wait_ge(out_done, 16 * n_out[0])

        @block.gpsimd
        def _(pool):
            step = Count(pool_step)
            pool.memset(SC[:, :, :], PAD_SCORE).then_inc(pads_set, 1)

            def lo(s, kc=KC):
                pool.wait_ge(hi_done, s + 1)
                pool.tensor_tensor(WLO[:, s % 2, 0:kc, :], RAW[:, s % 2, 0:kc, :], WHI[:, s % 2, 0:kc, :].bitcast(F32), ALU.subtract).then_inc(lo_done, 1)

            def lo_loop(g):
                with pool.Fori(0, g.iters) as i:
                    for j in range(2):
                        par = (g.slab0 + j) % 2
                        kc = g.kcs[j]
                        pool.wait_ge(hi_done, g.slab0 + 2 * i + j + 1)
                        pool.tensor_tensor(WLO[:, par, 0:kc, :], RAW[:, par, 0:kc, :], WHI[:, par, 0:kc, :].bitcast(F32), ALU.subtract).then_inc(lo_done, 1)

            def kidx(n):
                b = (4, 5, 6, 7, 0, 1, 2, 3)[n]
                if n == 0:
                    pool.wait_ge(pix_ready, 2)
                    pool.wait_ge(x_tr, 10)
                if n >= 4:
                    pool.wait_ge(kit_tr, 2 * (n - 3))
                src = t["cache_kidx"][0].rearrange("a (s p) d -> (a s) (p d)", s=SUB)
                pool.indirect_dma_start(KI[:, n % 4, :, :].rearrange("p a d -> p (a d)"), None, src, bass.IndirectOffsetOnAxis(ap=PIX[:, b:b + 1], axis=0)).then_inc(kidx_in[n % 4], 16)

            def cached(q):
                g, v, b = kv_order()[q]
                if q == 0:
                    pool.wait_ge(kit_tr, 16)
                if q >= 2:
                    if kv_order()[q - 2][1]:
                        pool.wait_ge(spv, sum(1 for x in kv_order()[:q - 1] if x[1]))
                    else:
                        pool.wait_ge(kts_tr, 4 * sum(1 for x in kv_order()[:q - 1] if not x[1]))
                src = t["cache_v" if v else "cache_k"][0].rearrange("a (s p) h d -> (a s) (p h d)", s=SUB)
                pool.indirect_dma_start(KN[:, q % 2, :, :].rearrange("p a d -> p (a d)"), None, src, bass.IndirectOffsetOnAxis(ap=PIX[:, b:b + 1], axis=0)).then_inc(kv_in[q % 2], 16)

            for s in range(2):
                lo(s)
            for n in range(4):
                kidx(n)
            for s in range(2, 5):
                lo(s)
            for i in range(1, NRB):
                m, nk = blk(i)
                pool.wait_ge(sc_done, IH * i)
                v = SC[0:m, i - 1, RB * i:RB * i + m]
                pool.affine_select(out=v, in_=v, pattern=[[-1, m]], compare_op=ALU.is_ge, fill=HIDDEN, base=0, channel_multiplier=1).then_inc(sc_masked, 1)
            for n in range(4, 8):
                kidx(n)
            for q in range(2):
                cached(q)
            pool.wait_ge(ss_done, 8)
            pool.wait_ge(qis_ready, 4)
            pool.memset(UE[:, :, 0:PB], 0.0).then_inc(u_zero, 1)
            for s in range(5, 8):
                lo(s)
            step.mark(pool.memset(NM[:, 0, 0:RB], 0.0))
            pool.wait_ge(pool_step, step.n)
            v = NM[:, 0, 0:RB]
            pool.affine_select(out=v, in_=v, pattern=[[-1, RB]], compare_op=ALU.is_ge, fill=NEG, base=0, channel_multiplier=1).then_inc(nm_final, 1)

            pool.wait_ge(acc_free[0], 8)
            pool.wait_ge(acc_free[1], 7)
            pool.wait_ge(sp_ready, 1)
            pool.wait_ge(comb_done, 10)
            for g in range(4):
                w = 2 << g
                src = UE[:, g, :]
                if g:
                    pool.wait_ge(pd_ready, g)
                for lev in range(g + 1):
                    sh, lo_x = 1 << lev, (2 << lev) - 1
                    dst = PA[:, lev % 2, :]
                    if step.n:
                        pool.wait_ge(pool_step, step.n)
                    step.mark(pool.tensor_tensor(dst[:, lo_x:UEW], src[:, lo_x:UEW], src[:, lo_x - sh:UEW - sh], ALU.add))
                    src = dst
                dst = PA[:, (g + 1) % 2, :]
                pool.wait_ge(pool_step, step.n)
                step.mark(pool.tensor_scalar(dst[:, PB:UEW], src[:, PB:UEW], 1.0 / w, None, ALU.mult))
                pool.wait_ge(pool_step, step.n)
                step.mark(pool.tensor_tensor(dst[:, PB:PB + 16], src[:, PB:PB + 16], CA[:, C_INV + 16 * g:C_INV + 16 * g + 16], ALU.mult))
                pool.wait_ge(pool_step, step.n)
                if g:
                    pool.wait_ge(y_done, g)
                pool.tensor_tensor(PD[:, 0:LP], dst[:, PB:EXT], UE[:, g, PB:EXT], ALU.subtract)
                tail = dst[:, EXT:UEW].rearrange("p (b x) -> p b x", x=SEG)[:, :, PB:SEG]
                utail = UE[:, g, EXT:UEW].rearrange("p (b x) -> p b x", x=SEG)[:, :, PB:SEG]
                pool.tensor_tensor(PD[:, LP:R].rearrange("p (b x) -> p b x", x=DT), tail, utail, ALU.subtract).then_inc(pd_ready, 1)
                if g == 0:
                    for i in range(1, NRB):
                        m, nk = blk(i)
                        pool.wait_ge(nm_ready, i)
                        v = NM[0:m, i, RB * i:RB * i + m]
                        pool.affine_select(out=v, in_=v, pattern=[[-1, m]], compare_op=ALU.is_ge, fill=NEG, base=0, channel_multiplier=1).then_inc(nm_final, 1)
            for q in range(2, 16):
                cached(q)
            for name in ("out0", "up0a", "down0a", "up0b", "down0b"):
                lo_loop(gemms[name])
            for sm, v in after(gemms["down0b"]):
                pool.wait_ge(sm, v)
            pool.memset(G[:, :, 0:LEAD], 0.0)
            pool.memset(LQ[:, :, :, :], 0.0)
            pool.memset(LK[:, :, :, :], 0.0)
            pool.memset(ATT[:, :, :], 0.0)
            pool.memset(BC[:, :, 0:LEAD], 0.0).then_inc(pads0, 1)
            lo(gemms["gd"].slab0)
            lo_loop(gemms["oq"])
            lo_loop(gemms["okv"])

            def split_heads(ap, size):
                return ap.rearrange("p h (b x) -> p h b x", x=size)

            for u in range(12):
                hp, n = divmod(u, 6)
                size = LEVELS[n]
                w = WP if n < 4 else GW
                if u == 0:
                    pool.wait_ge(pads0, 1)
                    pool.wait_ge(acc_free[0], gemms["okv"].use0 + 2)
                    pool.wait_ge(acc_free[1], gemms["okv"].use1 + 2)
                pool.wait_ge(lev_x, u + 1)
                if u >= 2:
                    pool.wait_ge(att_done, 7 * ((u - 2) // 6) + (u - 2) % 6 + 1)
                x = slice(0, size // 2)
                pool.tensor_tensor(split_heads(LK[:, u % 2, :, 0:w], size)[:, :, :, x], split_heads(G[:, 4 + 2 * hp:6 + 2 * hp, 0:w], size)[:, :, :, x],
                                   split_heads(LE[:, u % 2, :, 0:w], size)[:, :, :, x], ALU.mult).then_inc(lev_k, 1)
            for name in ("og", "out1", "up1a", "down1a", "up1b", "down1b"):
                lo_loop(gemms[name])

        @block.scalar
        def _(act):
            for g in range(NPG):
                act.dma_start(PTB[SUB * g:SUB * g + SUB, :], t["page_table"][g:g + 1, :].to_broadcast([SUB, DB])).then_inc(in_pt, 16)

            def hi(s):
                act.wait_ge(raw_in[s % 2], 16 * (s // 2 + 1))
                if s >= 2:
                    act.wait_ge(slab_used, s - 1)
                act.activation(WHI[:, s % 2, :, :], RAW[:, s % 2, :, :], ACT.Copy).then_inc(hi_done, 1)

            def hi_at(g, i, j):
                s = g.slab0 + j
                act.wait_ge(raw_in[s % 2], 16 * (s // 2 + 1) + 16 * i)
                act.wait_ge(slab_used, s - 1 + 2 * i)
                act.activation(WHI[:, s % 2, :, :], RAW[:, s % 2, :, :], ACT.Copy).then_inc(hi_done, 1)

            def norm(name):
                n = norm_no[name]
                for s, v in norms[n][1]:
                    act.wait_ge(s, v)
                for c in range(KC):
                    if KC * n + c >= 2:
                        act.wait_ge(sq_used, KC * n + c - 1)
                    act.activation(SQ[:, c % 2, :], XT[:, c, :], ACT.Square).then_inc(sq_ready, 1)
                act.wait_ge(sq_used, KC * (n + 1))
                act.activation(halved(RT), PS[:, 6:8, 0:HALF], ACT.Sqrt, bias=CA[:, C_EPS:C_EPS + 1]).then_inc(rt_ready, 1)
                if name == "final":
                    return
                for c in range(KC):
                    act.wait_ge(ht_ready, KC * n + c + 1)
                    act.activation(HHI[:, c, :], HT[:, c % 2, :], ACT.Copy).then_inc(hhi_ready, 1)

            hi(0)
            for g in range(1, 10, 2):
                act.wait_ge(x_tr, g + 1)
                i, c4 = g // 2, g % 2
                act.activation(XT[:, 4 * c4:4 * c4 + 4, RB * i:RB * i + RB], PS[:, g % 4, 0:4 * RB].rearrange("p (c r) -> p c r", c=4), ACT.Copy).then_inc(xe_a, 1)
            act.wait_ge(cols_ready, 1)
            norm("mix0")

            use = [0, 0]

            def evac(s, a, dst, src, last, scale=1.0):
                if a or s == 3:
                    act.wait_ge(slab_used, s + 1)
                else:
                    act.wait_ge(acc_done, use[0] + 1 - (s > 3))
                ins = act.activation(dst, src, ACT.Copy, scale=scale)
                if last:
                    ins.then_inc(acc_free[a], 1)
                    use[a] += 1

            for s in range(2):
                hi(s + 1)
                evac(s, 0, halved(QIT[:, 2 * s, :]), halves(0), True)
                use[1] += 1
            hi(3)
            evac(2, 0, halved(KT[:, :]), halves(0), False)
            evac(2, 0, halved(KX[64:128, :]), acc[0][0:64, :, 0:HALF], False)
            evac(2, 0, halved(KX[0:64, :]), acc[0][64:128, :, 0:HALF], True)
            use[1] += 1
            hi(4)
            evac(3, 0, halved(KID[0:64, :]), acc[0][0:64, :, 0:HALF], False)
            evac(3, 0, halved(KID[64:128, :]), acc[0][0:64, :, 0:HALF], False)
            evac(3, 0, halved(WIT[0:8, :]), acc[0][64:72, :, 0:HALF], True)
            for i in range(1, NRB):
                m, nk = blk(i)
                for h in range(IH):
                    n = IH * (i - 1) + h
                    act.wait_ge(il_ready, n + 1)
                    if n >= 2:
                        act.wait_ge(sc_done, n - 1)
                    act.activation(RL[0:m, n % 2, 0:nk].rearrange("p (a n) -> p a n", a=2), PS[0:m, 4 + 2 * (n % 2):6 + 2 * (n % 2), 0:nk // 2], ACT.Relu).then_inc(relu_done, 1)
            for gi, g in enumerate((1, 0)):
                for b4 in range(4):
                    n = 4 * gi + b4
                    for u in range(2):
                        act.wait_ge(kit_tr, 2 * n + u + 1)
                        if n >= 2:
                            act.wait_ge(ss_done, n - 1)
                        act.activation(KIT[:, n % 2, 512 * u:512 * u + 512], PS[:, 4 + u, :], ACT.Copy).then_inc(kit_ready, 1)
                act.wait_ge(ss_done, 4 * gi + 4)
                if gi:
                    act.wait_ge(comb_done, 5)
                pages = SR[:, 0:PAST].rearrange("p (x u j f) -> p u j f x", u=2, j=4, f=2)
                for u in range(2):
                    for hf in range(2):
                        act.activation(pages[:, u, :, hf, :], PS[:, 2 * u + hf, :].rearrange("p (j x) -> p j x", j=4), ACT.Relu).then_inc(sr_done, 1)
                act.activation(SR[:, PAST:SKEYS], PS[:, 6, 0:NS], ACT.Relu).then_inc(sr_done, 1)
                rows = NS if g else NS // 2
                for q in range(5):
                    w = 512 if q < 4 else NS
                    act.wait_ge(comb_done, 5 * gi + q + 1)
                    act.activation(SS[0:rows, 512 * q:512 * q + w], PS[0:rows, 7, 0:w], ACT.Copy).then_inc(comb_evac, 1)
            for s in range(4, 6):
                hi(s + 1)
                for j in range(2):
                    evac(s, j, halved(QT[:, 2 * (s - 4) + j, :]), halves(j), True, SCALE)
            for s in range(6, 8):
                hi(s + 1)
                for j in range(2):
                    g = 2 * (s - 6) + j
                    if g == 0:
                        act.wait_ge(u_zero, 1)
                    evac(s, j, UE[:, g, PB:PB + HALF], acc[j][:, 0, 0:HALF], False)
                    evac(s, j, UN[:, g, :], acc[j][:, 1, LP - HALF:HALF], False)
                    evac(s, j, UE[:, g, PB + HALF:EXT], acc[j][:, 1, 0:LP - HALF], False)
                    evac(s, j, UE[:, g, EXT:UEW].rearrange("p (b x) -> p b x", x=SEG)[:, :, PB:SEG],
                         acc[j][:, 1, LP - HALF:HALF].rearrange("p (b x) -> p b x", x=DT), True)
            act.wait_ge(sp_tr, 1)
            act.activation(UE[:, :, EXT:UEW].rearrange("p g (b x) -> p g b x", x=SEG)[:, :, :, 0:PB].rearrange("p g b x -> p g b x"),
                           PS[:, 6, 0:480].rearrange("p (g b x) -> p g b x", g=4, b=DB), ACT.Copy).then_inc(sp_ready, 1)
            for i in range(6):
                m = RB if i < 4 else (LAST if i == 4 else NS)
                act.wait_ge(kvr_tr, i + 1)
                act.activation(KVR[0:m, i, :], PS[0:m, 4 + i % 2, 0:320], ACT.Copy).then_inc(kvr_ready, 1)
            for j, m in enumerate((PB, NS)):
                act.wait_ge(uo_tr, j + 1)
                act.activation(UO[0:m, j, :], PS[0:m, 6 + j, :], ACT.Copy).then_inc(uo_ready, 1)
            act.wait_ge(in_consts, 16)

            def exps(n):
                i, h = divmod(n, NH)
                m, nk = blk(i)
                act.wait_ge(mx_ready, n + 1)
                if n >= 2:
                    act.wait_ge(pt_tr, n - 1)
                act.activation(PR[0:m, n % 2, 0:nk].rearrange("p (a n) -> p a n", a=2), PS[0:m, 4 + 2 * (n % 2):6 + 2 * (n % 2), 0:nk // 2],
                               ACT.Exp, bias=ST[0:m, 0, n:n + 1], accum_out=ST[0:m, 1, n:n + 1]).then_inc(exp_done, 1)

            def pt_copy(n):
                i, h = divmod(n, NH)
                m, nk = blk(i)
                act.wait_ge(pt_tr, n + 1)
                if n >= 2:
                    act.wait_ge(pv_done, n - 1)
                full = min(i + 1, 4)
                ins = act.activation(PT[:, n % 2, 0:full, 0:m], PS[0:RB, 0, 0:full * RB].rearrange("p (j r) -> p j r", j=full)[:, :, 0:m], ACT.Copy)
                if i == 4:
                    ins = act.activation(PT[0:LAST, n % 2, 4, 0:m], PS[0:LAST, 1, 0:m], ACT.Copy)
                ins.then_inc(pt_evac, 1)

            def o_hi(n):
                i, h = divmod(n, NH)
                m, nk = blk(i)
                act.wait_ge(pv_done, n + 1)
                act.activation(HHI[:, h // 2, RB * i:RB * i + m], PS[:, 2 + (n // 2) % 2, 0:m], ACT.Copy).then_inc(ohi, 1)

            NST = NRB * NH
            exps(0)
            for n in range(NST):
                if n + 1 < NST:
                    exps(n + 1)
                pt_copy(n)
                if n % 2 == 0 and n:
                    o_hi(n - 1)
                if n % NH == NH - 1 and n // NH < 4:
                    g = n // NH
                    act.wait_ge(y_done, g + 1)
                    act.activation(halved(HHI[:, 4 + g, :]), PS[:, 0:2, 0:HALF], ACT.Copy, scale=COLS[:, COL_PS + g:COL_PS + g + 1]).then_inc(yhi, 1)
            o_hi(NST - 1)

            ce = Count(kts_evac)
            for g in range(2):
                for b4 in range(4):
                    nb = 4 * g + b4
                    for u in range(4):
                        if u % 2 == 0:
                            act.wait_ge(kts_tr, 4 * nb + u + 1)
                            if nb and u == 0:
                                act.wait_ge(slg, nb)
                            if nb == 0 and u == 0:
                                act.wait_ge(ss_done, 8)
                            act.activation(KTS[:, 512 * u:512 * u + 512], PS[:, 6 + u % 2, :], ACT.Copy).then_inc(kts_evac, 1)
                act.wait_ge(smx, 3 * g + 3)
                act.activation(SR[:, 0:PAST], PS[:, 0:4, :].rearrange("p a n -> p (a n)"), ACT.Exp, bias=STS[:, 2:3], accum_out=STS[:, 3:4])
                act.activation(SR[:, PAST:SKEYS], PS[:, 4, 0:NS], ACT.Exp, bias=STS[:, 2:3], accum_out=STS[:, 4:5]).then_inc(sexp, 1)
                for u in range(5):
                    if u % 2 == 0:
                        act.wait_ge(spt_tr, 5 * g + u + 1)
                        if u < 4:
                            act.activation(PTS[:, 4 * u:4 * u + 4, :], PS[:, 6, :].rearrange("p (j r) -> p j r", j=4), ACT.Copy).then_inc(spt_evac, 1)
                        else:
                            act.activation(PTS[0:NS, TOK, :], PS[0:NS, 6, 0:P], ACT.Copy).then_inc(spt_evac, 1)
                act.wait_ge(spv, 4 * g + 4)
                src = PS[:, 5, 0:P].rearrange("p (b k h t) -> p k h b t", b=4, k=2, h=GRP)
                for kv in range(2):
                    for par in range(2):
                        for c in range(2):
                            act.activation(HHI[64 * par:64 * par + 64, 2 * kv + c, LP + 16 * g:LP + 16 * g + 16].rearrange("p (b t) -> p b t", b=4),
                                           src[64 * kv:64 * kv + 64, kv, 2 * c + par, :, :], ACT.Copy).then_inc(sohi, 1)

            def out_rows(g, final=False):
                with act.Fori(0, g.iters - final) as i:
                    hi_at(g, i, 1)
                    hi_at(g, i, 2)
                if final:
                    hi_at(g, g.iters - 1, 1)

            def up_rows(g):
                with act.Fori(0, g.iters) as i:
                    hi_at(g, i, 1)
                    for j in range(2):
                        act.wait_ge(*tile_done(g, j, 2 * i, 2 * i))
                        act.activation(halved(SG[:, j, :]), halves(j), ACT.Silu).then_inc(acc_free[j], 1)
                    hi_at(g, i, 2)
                    for j in range(2):
                        act.wait_ge(acc_free[j], (g.use0, g.use1)[j] + 2 * i + 2)
                        act.activation(AHI[:, ds(2 * i + j, 1), :].rearrange("p a n -> p (a n)"), AT[:, j, :], ACT.Copy).then_inc(ahi_ready, 1)

            out_rows(gemms["out0"])
            norm("ffn0")
            for name in ("up0a", "down0a", "up0b", "down0b"):
                g = gemms[name]
                (up_rows if g.kind == "up" else out_rows)(g)
            norm("mix1")
            gd = gemms["gd"]
            hi(gd.slab0 + 1)
            act.wait_ge(slab_used, gd.slab0 + 1)
            act.activation(halved(GD[:, :]), acc[0][0:16, :, 0:HALF], ACT.Copy).then_inc(acc_free[0], 1)

            def odd_rows(g, t0, scale=1.0):
                with act.Fori(0, g.iters) as i:
                    for q in range(2):
                        hi_at(g, i, q + 1)
                        act.wait_ge(*tile_done(g, 0, 2 * i + q, 2 * i + q))
                        act.activation(G[:, ds(t0 + 4 * i + 2 * q, 1), LEAD:GW].rearrange("p a (h n) -> p (a h) n", h=2), halves(0), ACT.Copy, scale=scale).then_inc(acc_free[0], 1)

            act.wait_ge(pads0, 1)
            odd_rows(gemms["oq"], 0, GDK ** -0.5)
            for h in range(GH):
                L = GSC[:, h % 2, :]
                act.wait_ge(la_mm, h + 1)
                if h >= 2:
                    act.wait_ge(la_sub, h - 1)
                act.activation(halved(L), PS[:, 4 + 2 * (h % 2):6 + 2 * (h % 2), 0:HALF], ACT.Abs, bias=COLS[:, COL_BG + h:COL_BG + h + 1]).then_inc(la_abs, 1)
                act.wait_ge(la_abs, h + 1)
                act.activation(L, L, ACT.Exp, scale=-1.0).then_inc(la_act, 1)
                act.wait_ge(la_act, 2 * h + 1)
                act.activation(L, L, ACT.Ln, bias=1.0).then_inc(la_act, 1)
            odd_rows(gemms["okv"], 4)
            for u in range(12):
                n = u % 6
                w = WP if n < 4 else GW
                act.wait_ge(lev_e, u + 1)
                v = LE[:, u % 2, :, 0:w]
                act.activation(v, v, ACT.Exp, scale=1.0 / GNORM).then_inc(lev_x, 1)
            act.wait_ge(b_ready, GH)
            act.activation(EB[:, :, 0:NCP], BC[:, :, CH - 1:WP:CH], ACT.Exp, scale=1.0 / GNORM)
            act.activation(EB[:, :, NCP:NCP + DB], BC[:, :, WP + DT - 1:GW:DT], ACT.Exp, scale=1.0 / GNORM).then_inc(eb_ready, 1)
            for hp in range(2):
                act.wait_ge(kh_e, hp + 1)
                act.activation(LE[:, hp, :, :], LE[:, hp, :, :], ACT.Exp, scale=1.0 / GNORM).then_inc(kh_x, 1)
                act.wait_ge(att_done, 14)
                act.wait_ge(lev_q, 12)
                act.activation(LQ[:, hp, :, :], BC[:, 2 * hp:2 * hp + 2, :], ACT.Exp, scale=1.0 / GNORM).then_inc(qe_x, 1)
            for c in range(NCH):
                m = CH if c < NCP else NS
                act.wait_ge(vk_tr, c + 1)
                if c >= 2:
                    act.wait_ge(o_done, c - 1)
                for par in range(2):
                    act.activation(VR[64 * par:64 * par + m, c % 2, :], PS[0:m, par, :], ACT.Copy)
                for par in range(2):
                    ins = act.activation(KR[64 * par:64 * par + m, c % 2, :], PS[0:m, 2, 2 * GDK * par:2 * GDK * par + 2 * GDK], ACT.Copy)
                ins.then_inc(vk_ev, 1)
            def head_root(h):
                act.wait_ge(osq_used, 2 * h + 2)
                act.activation(halved(GRR[:, h, :]), PS[:, 4 + 2 * (h % 2):6 + 2 * (h % 2), 0:HALF], ACT.Sqrt, bias=CA[:, C_EPS:C_EPS + 1]).then_inc(ort, 1)

            for h in range(GH):
                for e in range(2):
                    n = 2 * h + e
                    act.wait_ge(oi_ev, 1)
                    if n >= 2:
                        act.wait_ge(osq_used, n - 1)
                    act.activation(GSC[:, n % 2, :], G[:, 8 + n, LEAD:GW], ACT.Square).then_inc(osq_ready, 1)
                if h:
                    head_root(h - 1)
            head_root(GH - 1)
            g = gemms["og"]
            for i in range(2):
                for q in range(2):
                    hi_at(g, i, q + 1)
                    n = 2 * i + q
                    for j in range(2):
                        act.wait_ge(*tile_done(g, j, n, n))
                        if n:
                            act.wait_ge(gate_ready, 2 * (n - 1) + j + 1)
                        else:
                            act.wait_ge(osq_used, 8)
                        act.activation(halved(GSC[:, j, :]), halves(j), ACT.Silu).then_inc(acc_free[j], 1)
            for c in range(KC):
                act.wait_ge(gate_ready, c + 1)
                act.wait_ge(slab_used, g.slab0 + 4)
                act.activation(HHI[:, c, :], G[:, 8 + c, LEAD:GW], ACT.Copy).then_inc(o2hi, 1)
            out_rows(gemms["out1"])
            norm("ffn1")
            for name in ("up1a", "down1a", "up1b", "down1b"):
                g = gemms[name]
                up_rows(g) if g.kind == "up" else out_rows(g, name == "down1b")
            norm("final")
            for n in range(1, 2 * NRB, 2):
                act.wait_ge(y_tr, n + 1)
                if n >= 4:
                    act.wait_ge(yr_out[n % 4], yr_total(n % 4, n - 3))
                act.wait_ge(yr_ready, n)
                act.activation(YR[:, n % 4, :], PS[0:RB, n % 4, :], ACT.Copy).then_inc(yr_ready, 1)

        @block.vector
        def _(dve):
            dve.wait_ge(in_pt, 16 * NPG)
            dve.tensor_copy(PTF[:, :], PTB[:, :]).then_inc(pix_ready, 1)
            dve.wait_ge(in_consts, 16)
            dve.wait_ge(pix_ready, 1)
            dve.tensor_scalar(PIX[:, :], PTF[:, :], float(SUB), CA[:, C_SUB:C_SUB + 1], ALU.mult, ALU.add).then_inc(pix_ready, 1)
            dve.wait_ge(vec_tr, 1)
            dve.tensor_copy(COLS[:, :], PS[:, 4, 0:50]).then_inc(cols_ready, 1)
            for g in range(0, 10, 2):
                dve.wait_ge(x_tr, g + 1)
                i, c4 = g // 2, g % 2
                dve.tensor_copy(XT[:, 4 * c4:4 * c4 + 4, RB * i:RB * i + RB], PS[:, g % 4, 0:4 * RB].rearrange("p (c r) -> p c r", c=4)).then_inc(xe_d, 1)
            dve.tensor_copy(IDB[:, :], IDN)
            dve.tensor_copy(EXB[:, :, :], CA[0:NS, C_EX:C_EX + 2 * P].rearrange("p (g n) -> p g n", g=2)).then_inc(casts, 1)

            def norm(name):
                n, col = norm_no[name], norm_cols[name]
                dve.wait_ge(rt_ready, n + 1)
                dve.reciprocal(RR, RT).then_inc(rr_ready, 1)
                dve.wait_ge(rr_ready, n + 1)
                for s, v in norms[n][1]:
                    dve.wait_ge(s, v)

                def ht(c):
                    if KC * n + c >= 2:
                        dve.wait_ge(h_ready, KC * n + c - 1)
                    dve.scalar_tensor_tensor(HT[:, c % 2, :], XT[:, c, :], COLS[:, col + c:col + c + 1], RR, ALU.mult, ALU.mult).then_inc(ht_ready, 1)

                def lo(c):
                    dve.wait_ge(hhi_ready, KC * n + c + 1)
                    dve.tensor_tensor(HLO[:, c, :], HT[:, c % 2, :], HHI[:, c, :].bitcast(F32), ALU.subtract).then_inc(h_ready, 1)

                dve.wait_ge(cols_ready, 1)
                if name == "final":
                    for c in range(KC):
                        dve.scalar_tensor_tensor(XT[:, c, :], XT[:, c, :], COLS[:, col + c:col + c + 1], RR, ALU.mult, ALU.mult).then_inc(ht_ready, 1)
                    return
                ht(0)
                for c in range(KC):
                    if c + 1 < KC:
                        ht(c + 1)
                    lo(c)

            norm("mix0")
            for s in range(2):
                dve.wait_ge(slab_used, s + 1)
                dve.tensor_copy(halved(QIT[:, 2 * s + 1, :]), halves(1)).then_inc(acc_free[1], 1)
            dve.wait_ge(acc_free[0], 2)
            dve.wait_ge(acc_free[1], 2)
            for hf in range(2):
                for par in range(2):
                    dve.tensor_copy(QIS[64 * hf:64 * hf + 64, :, :, :].rearrange("p b (c f) t -> p b c f t", f=2)[:, :, :, par, :],
                                    QIT[64 * par:64 * par + 64, :, LP:R].rearrange("p c (b t) -> p b c t", b=DB)).then_inc(qis_ready, 1)
            dve.wait_ge(slab_used, 3)
            dve.tensor_copy(halved(VT[:, :]), halves(1)).then_inc(acc_free[1], 1)
            dve.wait_ge(wi_tr, 1)
            dve.tensor_copy(WIR[:, 0:4, :], PS[0:RB, 4, 0:32].rearrange("p (i h) -> p i h", i=4))
            dve.tensor_copy(WIR[0:LAST, 4, :], PS[0:LAST, 4, 32:40]).then_inc(wir_ready, 1)
            for g in range(2):
                dve.tensor_tensor(WSEL[:, g, :], PS[:, 5, 0:NS], CA[:, C_DM + NS * g:C_DM + NS * g + NS], ALU.mult).then_inc(wsel_ready, 1)
            dve.wait_ge(wir_ready, 1)
            dve.wait_ge(pads_set, 1)
            for i in range(1, NRB):
                m, nk = blk(i)
                for h in range(IH):
                    n = IH * (i - 1) + h
                    dve.wait_ge(relu_done, n + 1)
                    s = SC[0:m, i - 1, 0:nk]
                    w = WIR[0:m, i, h:h + 1]
                    if h == 0:
                        dve.tensor_scalar(s, RL[0:m, n % 2, 0:nk], w, None, ALU.mult).then_inc(sc_done, 1)
                    else:
                        dve.wait_ge(sc_done, n)
                        dve.scalar_tensor_tensor(s, RL[0:m, n % 2, 0:nk], w, s, ALU.mult, ALU.add).then_inc(sc_done, 1)
            dve.wait_ge(sc_masked, 4)

            def top8(i, before):
                m, nk = blk(i)
                if before is not None:
                    dve.wait_ge(tk, before)
                dve.max(M8[0:m, i - 1, :], SC[0:m, i - 1, 0:nk + PADS]).then_inc(tk, 1)

            def take8(i, found):
                m, nk = blk(i)
                s = SC[0:m, i - 1, 0:nk + PADS]
                dve.wait_ge(tk, found)
                dve.match_replace(out=s, in_to_replace=M8[0:m, i - 1, :], in_values=s, imm_value=TAKEN).then_inc(tk, 1)

            for i in range(1, NRB):
                top8(i, None)
            for i in range(1, NRB):
                take8(i, i)
            for r in range(1, ROUNDS_P):
                for i in range(1, NRB):
                    top8(i, 8 * r - 4 + i)
                for i in range(1, NRB):
                    take8(i, 8 * r + i)
            for i in range(1, NRB):
                m, nk = blk(i)
                dve.wait_ge(tk, 8 * ROUNDS_P)
                dve.tensor_scalar(NM[0:m, i, 0:nk], SC[0:m, i - 1, 0:nk], TAKEN_CUT, NEG, ALU.is_gt, ALU.mult).then_inc(nm_ready, 1)
            dve.wait_ge(comb_evac, 10)
            dve.tensor_tensor(SS[:, PAST:SKEYS], SS[:, PAST:SKEYS], CA[0:NS, C_VN:C_VN + NS], ALU.mult).then_inc(newscore, 1)
            dve.wait_ge(newscore, 1)
            dve.tensor_tensor(SS[:, PAST:SKEYS], SS[:, PAST:SKEYS], CA[0:NS, C_FN:C_FN + NS], ALU.add).then_inc(newscore, 1)
            dve.memset(QBD[:, :, :, :], 0.0).then_inc(qbd_ready, 1)
            dve.wait_ge(qbd_ready, 1)
            dve.wait_ge(acc_free[0], 6)
            dve.wait_ge(acc_free[1], 5)
            for kv in range(2):
                for hh in range(GRP):
                    h = kv * GRP + hh
                    dve.tensor_copy(QBD[64 * kv:64 * kv + 64, :, kv, DT * hh:DT * hh + DT],
                                    QT[64 * (h % 2):64 * (h % 2) + 64, h // 2, LP:R].rearrange("p (b t) -> p b t", b=DB)).then_inc(qbd_ready, 1)

            def sample_round(r):
                if r:
                    dve.wait_ge(tks, 2 * r)
                else:
                    dve.wait_ge(newscore, 2)
                dve.max(M8S[:, :], SS[:, :]).then_inc(tks, 1)
                dve.wait_ge(tks, 2 * r + 1)
                dve.match_replace(out=SS[:, :], in_to_replace=M8S[:, :], in_values=SS[:, :], imm_value=TAKEN).then_inc(tks, 1)

            def row_max(n):
                i, h = divmod(n, NH)
                m, nk = blk(i)
                dve.wait_ge(lg_ready, n + 1)
                dve.tensor_reduce(ST[0:m, 0, n:n + 1], PS[0:m, 4 + 2 * (n % 2):6 + 2 * (n % 2), 0:nk // 2], AX.XY, ALU.max, negate=True).then_inc(mx_ready, 1)

            def scale_rows(n):
                i, h = divmod(n, NH)
                m, nk = blk(i)
                dve.wait_ge(exp_done, n + 1)
                dve.reciprocal(ST[0:m, 2, n:n + 1], ST[0:m, 1, n:n + 1]).then_inc(rinv, 1)
                dve.wait_ge(rinv, n + 1)
                v = PR[0:m, n % 2, 0:nk]
                dve.tensor_scalar(v, v, ST[0:m, 2, n:n + 1], None, ALU.mult).then_inc(pr_ready, 1)

            def o_lo(n):
                i, h = divmod(n, NH)
                m, nk = blk(i)
                dve.wait_ge(ohi, n // 2 + 1)
                dst = HLO[:, h // 2, RB * i:RB * i + m]
                dve.tensor_tensor(dst, PS[:, 2 + (n // 2) % 2, 0:m], HHI[:, h // 2, RB * i:RB * i + m].bitcast(F32), ALU.subtract).then_inc(olo, 1)

            NST = NRB * NH
            row_max(0)
            for n in range(NST):
                if n + 1 < NST:
                    row_max(n + 1)
                scale_rows(n)
                if n % 2 == 1 and n >= 3:
                    o_lo(n - 2)
                if n % NH == NH - 1 and n // NH < 4:
                    g = n // NH
                    dve.wait_ge(yhi, g + 1)
                    dve.scalar_tensor_tensor(halved(HLO[:, 4 + g, :]), PS[:, 0:2, 0:HALF], COLS[:, COL_PS + g:COL_PS + g + 1],
                                             halved(HHI[:, 4 + g, :].bitcast(F32)), ALU.mult, ALU.subtract).then_inc(ylo, 1)
                if n < ROUNDS_S:
                    sample_round(n)
            o_lo(NST - 1)
            dve.wait_ge(tks, 2 * ROUNDS_S)
            dve.tensor_scalar(NMS[:, :], SS[:, :], TAKEN_CUT, NEG, ALU.is_gt, ALU.mult).then_inc(nms_ready, 1)

            for g in range(2):
                for b4 in range(4):
                    nb = 4 * g + b4
                    for u in range(4):
                        if u % 2:
                            dve.wait_ge(kts_tr, 4 * nb + u + 1)
                            if nb and u == 1:
                                dve.wait_ge(slg, nb)
                            dve.tensor_copy(KTS[:, 512 * u:512 * u + 512], PS[:, 6 + u % 2, :]).then_inc(kts_evac2, 1)
                dve.wait_ge(slg, 4 * g + 4)
                dve.wait_ge(slg_mask, g + 1)
                dve.tensor_reduce(STS[:, 0:1], PS[:, 0:4, :], AX.XY, ALU.max, negate=True).then_inc(smx, 1)
                dve.tensor_reduce(STS[:, 1:2], PS[:, 4, 0:NS], AX.X, ALU.max, negate=True).then_inc(smx, 1)
                dve.wait_ge(smx, 3 * g + 2)
                dve.tensor_tensor(STS[:, 2:3], STS[:, 0:1], STS[:, 1:2], ALU.min).then_inc(smx, 1)
                dve.wait_ge(sexp, g + 1)
                dve.tensor_tensor(STS[:, 5:6], STS[:, 3:4], STS[:, 4:5], ALU.add).then_inc(sstat, 1)
                dve.wait_ge(sstat, 2 * g + 1)
                dve.reciprocal(STS[:, 6:7], STS[:, 5:6]).then_inc(sstat, 1)
                dve.wait_ge(sstat, 2 * g + 2)
                dve.tensor_scalar(SR[:, :], SR[:, :], STS[:, 6:7], None, ALU.mult).then_inc(sp_norm, 1)
                for u in (1, 3):
                    dve.wait_ge(spt_tr, 5 * g + u + 1)
                    dve.tensor_copy(PTS[:, 4 * u:4 * u + 4, :], PS[:, 7, :].rearrange("p (j r) -> p j r", j=4)).then_inc(spt_evac2, 1)
                src = PS[:, 5, 0:P].rearrange("p (b k h t) -> p k h b t", b=4, k=2, h=GRP)
                dve.wait_ge(sohi, 8 * g + 8)
                for kv in range(2):
                    for par in range(2):
                        for c in range(2):
                            dst = (slice(64 * par, 64 * par + 64), 2 * kv + c, slice(LP + 16 * g, LP + 16 * g + 16))
                            dve.tensor_tensor(HLO[dst].rearrange("p (b t) -> p b t", b=4), src[64 * kv:64 * kv + 64, kv, 2 * c + par, :, :],
                                              HHI[dst].bitcast(F32).rearrange("p (b t) -> p b t", b=4), ALU.subtract).then_inc(solo, 1)

            def residual_rows(g):
                pairs = 2 if g.kind == "out" else 1
                with dve.Fori(0, g.iters) as i:
                    for q in range(pairs):
                        for j in range(2):
                            dve.wait_ge(*(tile_done(g, j, 2 * i + q, 2 * i + q) if pairs == 2 else tile_done(g, j, i, 2 * i + 1)))
                            x = XT[:, ds(2 * pairs * i + 2 * q + j, 1), :].rearrange("p a (h n) -> p (a h) n", h=2)
                            dve.tensor_tensor(x, halves(j), x, ALU.add).then_inc(acc_free[j], 1)

            def new_states(b):
                dve.wait_ge(su_done, b + 1)
                dve.wait_ge(st_in[b % 2], 16 * (b // 2 + 1))
                if b >= 2:
                    dve.wait_ge(st_out[b % 2], 16 * (b // 2))
                bank = 5 if b % 2 else 0
                for h in range(GH):
                    u = PS[:, bank + h % 2, GDV * (h // 2):GDV * (h // 2) + GDV]
                    dve.scalar_tensor_tensor(SNEW[:, b % 2, h, :], SIN[:, b % 2, h, :], EB[:, h, NCP + b:NCP + b + 1], u, ALU.mult, ALU.add).then_inc(sn_ready, 1)

            def up_rows(g):
                with dve.Fori(0, g.iters) as i:
                    dve.wait_ge(alo_ready, a0[g] + 2 * i + 1)
                    for j in range(2):
                        use = (g.use0, g.use1)[j] + 2 * i
                        dve.wait_ge(*tile_done(g, j, 2 * i + 1, 2 * i + 1))
                        dve.wait_ge(acc_free[j], use + 1)
                        dve.tensor_tensor(halved(AT[:, j, :]), halves(j), halved(SG[:, j, :]), ALU.mult).then_inc(acc_free[j], 1)
                    for j in range(2):
                        dve.wait_ge(ahi_ready, a0[g] + 2 * i + j + 1)
                        hi = AHI[:, ds(2 * i + j, 1), :].rearrange("p a n -> p (a n)").bitcast(F32)
                        dve.tensor_tensor(ALO[:, ds(2 * i + j, 1), :].rearrange("p a n -> p (a n)"), AT[:, j, :], hi, ALU.subtract).then_inc(alo_ready, 1)

            residual_rows(gemms["out0"])
            norm("ffn0")
            dve.memset(AT[:, 0, 0:1], 0.0).then_inc(alo_ready, 1)
            for name in ("up0a", "down0a", "up0b", "down0b"):
                g = gemms[name]
                (up_rows if g.kind == "up" else residual_rows)(g)
            norm("mix1")

            def odd_rows(g, t0, scale=1.0):
                with dve.Fori(0, g.iters) as i:
                    for q in range(2):
                        dve.wait_ge(*tile_done(g, 1, 2 * i + q, 2 * i + q))
                        dve.tensor_scalar(G[:, ds(t0 + 4 * i + 2 * q + 1, 1), LEAD:GW].rearrange("p a (h n) -> p (a h) n", h=2), halves(1), scale, None, ALU.mult).then_inc(acc_free[1], 1)

            dve.wait_ge(pads0, 1)
            odd_rows(gemms["oq"], 0, GDK ** -0.5)
            dve.wait_ge(in_cg, 16)
            for h in range(GH):
                v = BC[:, h, LEAD:GW]
                dve.wait_ge(la_abs, h + 1)
                dve.tensor_scalar(halved(v), PS[:, 4 + 2 * (h % 2):6 + 2 * (h % 2), 0:HALF], COLS[:, COL_BG + h:COL_BG + h + 1], 0.0, ALU.add, ALU.min).then_inc(la_min, 1)
                dve.wait_ge(la_min, h + 1)
                dve.wait_ge(la_act, 2 * h + 2)
                dve.tensor_tensor(v, v, GSC[:, h % 2, :], ALU.subtract).then_inc(la_sub, 1)
            for h in range(GH):
                dve.wait_ge(la_sub, h + 1)
                dve.tensor_tensor_scan(BC[:, h, :], CG[:, G_RST:G_RST + GW], BC[:, h, :], 0.0, ALU.mult, ALU.add).then_inc(b_ready, 1)
            odd_rows(gemms["okv"], 4)

            def blocks(ap, size):
                return ap.rearrange("p h (b x) -> p h b x", x=size)

            def level_exponents(u):
                hp, n = divmod(u, 6)
                size = LEVELS[n]
                w = WP if n < 4 else GW
                half = size // 2
                b = blocks(BC[:, 2 * hp:2 * hp + 2, 0:w], size)
                e = blocks(LE[:, u % 2, :, 0:w], size)
                mid = b[:, :, :, half - 1:half].to_broadcast([P, 2, w // size, half])
                if u == 0:
                    dve.wait_ge(b_ready, GH)
                if u >= 2:
                    dve.wait_ge(lev_k, u - 1)
                    dve.wait_ge(lev_q, u - 1)
                dve.tensor_tensor(e[:, :, :, 0:half], mid, b[:, :, :, 0:half], ALU.subtract)
                dve.tensor_tensor(e[:, :, :, half:size], b[:, :, :, half:size], mid, ALU.subtract).then_inc(lev_e, 1)

            def level_queries(u):
                hp, n = divmod(u, 6)
                size = LEVELS[n]
                w = WP if n < 4 else GW
                x = slice(size // 2, size)
                dve.wait_ge(lev_x, u + 1)
                if u >= 2:
                    dve.wait_ge(att_done, 7 * ((u - 2) // 6) + (u - 2) % 6 + 1)
                dve.tensor_tensor(blocks(LQ[:, u % 2, :, 0:w], size)[:, :, :, x], blocks(G[:, 2 * hp:2 * hp + 2, 0:w], size)[:, :, :, x],
                                  blocks(LE[:, u % 2, :, 0:w], size)[:, :, :, x], ALU.mult).then_inc(lev_q, 1)

            def attention_part(v):
                hp, n = divmod(v, 7)
                dve.wait_ge(att_done, v + 1)
                bank = 4 + 2 * (v % 2)
                ps = PS[:, bank:bank + 2, :].rearrange("p a n -> p (a n)")
                mask = CG[:, G_MASK + CH * n:G_MASK + CH * n + CH].bitcast(I32)
                ins = dve.copy_predicated(ATT[:, hp, 0:WP].rearrange("p (c q) -> p c q", q=CH), mask.unsqueeze(1).to_broadcast([P, NCP, CH]),
                                          ps[:, 0:WP].rearrange("p (c q) -> p c q", q=CH))
                if n >= 4:
                    for par in range(2):
                        rows = slice(64 * par, 64 * par + NS)
                        ins = dve.copy_predicated(ATT[rows, hp, WP:GW], mask[rows, 0:NS], ps[rows, WP:GW])
                ins.then_inc(att_ev, 1)

            level_exponents(0)
            for u in range(12):
                if u + 1 < 12:
                    level_exponents(u + 1)
                level_queries(u)
                hp, n = divmod(u, 6)
                for v in {0: (), 6: (5, 6)}.get(u, (7 * hp + n - 1,)):
                    if v:
                        dve.wait_ge(att_ev, v)
                    attention_part(v)
            for v in (12, 13):
                dve.wait_ge(att_ev, v)
                attention_part(v)
            for hp in range(2):
                b = BC[:, 2 * hp:2 * hp + 2, :]
                if hp == 0:
                    dve.wait_ge(lev_k, 12)
                    dve.wait_ge(lev_q, 12)
                for w0, w1, size in ((0, WP, CH), (WP, GW, DT)):
                    bb = blocks(b[:, :, w0:w1], size)
                    end = bb[:, :, :, size - 1:size].to_broadcast([P, 2, (w1 - w0) // size, size])
                    ins = dve.tensor_tensor(blocks(LE[:, hp, :, w0:w1], size), end, bb, ALU.subtract)
                ins.then_inc(kh_e, 1)
            dve.wait_ge(att_done, 14)
            for hp in range(2):
                dve.wait_ge(kh_x, hp + 1)
                k = G[:, 4 + 2 * hp:6 + 2 * hp, :]
                dve.tensor_tensor(k, k, LE[:, hp, :, :], ALU.mult).then_inc(kh_ready, 1)
                dve.wait_ge(qe_x, hp + 1)
                q = G[:, 2 * hp:2 * hp + 2, :]
                dve.tensor_tensor(q, q, LQ[:, hp, :, :], ALU.mult).then_inc(qe_ready, 1)
            dve.wait_ge(eb_ready, 1)

            def chunk_out(c):
                dve.wait_ge(o_done, c + 1)
                m = CH if c < NCP else NS
                for par in range(2):
                    dst = G[:, 8:16, CH * c:CH * c + m].rearrange("p (a par e) n -> p par a e n", par=2, e=2)
                    ins = dve.tensor_copy(dst[:, par], PS[:, 3 + par, 0:4 * m].rearrange("p (a e n) -> p a e n", a=2, e=2))
                ins.then_inc(o_ev, 1)

            for c in range(NCP):
                dve.wait_ge(u_done, c + 1)
                if c >= 2:
                    dve.wait_ge(o_done, c)
                for h in range(GH):
                    u = PS[:, 5 + h % 2, GDV * (h // 2):GDV * (h // 2) + GDV]
                    dst = STATE[:, (c + 1) % 2, h, :]
                    if c == 0:
                        dve.tensor_copy(dst, u).then_inc(s_new, 1)
                    else:
                        dve.wait_ge(s_new, GH * (c - 1) + h + 1)
                        dve.scalar_tensor_tensor(dst, STATE[:, c % 2, h, :], EB[:, h, c:c + 1], u, ALU.mult, ALU.add).then_inc(s_new, 1)
                chunk_out(c)
            dve.wait_ge(vk_ev, NCH)
            for b in range(DB):
                if b >= 2:
                    dve.wait_ge(su_done, b - 1)
                dve.tensor_scalar(KB[:, b % 2, :], KR[0:96, NCP % 2, :], CG[0:96, G_SB + b:G_SB + b + 1], None, ALU.mult).then_inc(kb_ready, 1)
                if b == 0:
                    chunk_out(NCP)
                if b:
                    new_states(b - 1)
            new_states(DB - 1)
            dve.wait_ge(o_ev, NCH)
            dve.wait_ge(oi_done, DB)
            v = G[:, 8:16, WP:GW]
            dve.tensor_tensor(v, v, PS[:, 7, 0:256].rearrange("p (a n) -> p a n", a=8), ALU.add).then_inc(oi_ev, 1)
            for h in range(GH):
                dve.wait_ge(ort, h + 1)
                dve.reciprocal(GRR[:, h, :], GRR[:, h, :]).then_inc(orr, 1)
            g = gemms["og"]
            for h in range(GH):
                for j in range(2):
                    n = 2 * h + j
                    v = G[:, 8 + n, LEAD:GW]
                    dve.wait_ge(orr, h + 1)
                    dve.scalar_tensor_tensor(v, v, COLS[:, COL_GN + j:COL_GN + j + 1], GRR[:, h, :], ALU.mult, ALU.mult).then_inc(osc, 1)
                for j in range(2):
                    n = 2 * h + j
                    v = G[:, 8 + n, LEAD:GW]
                    dve.wait_ge(osc, n + 1)
                    dve.wait_ge(acc_free[j], (g.use0, g.use1)[j] + h + 1)
                    dve.tensor_tensor(v, v, GSC[:, j, :], ALU.mult).then_inc(gate_ready, 1)
            for c in range(KC):
                dve.wait_ge(o2hi, c + 1)
                dve.tensor_tensor(HLO[:, c, :], G[:, 8 + c, LEAD:GW], HHI[:, c, :].bitcast(F32), ALU.subtract).then_inc(o2lo, 1)
            residual_rows(gemms["out1"])
            norm("ffn1")
            for name in ("up1a", "down1a", "up1b", "down1b"):
                g = gemms[name]
                (up_rows if g.kind == "up" else residual_rows)(g)
            norm("final")
            for n in range(0, 2 * NRB, 2):
                dve.wait_ge(y_tr, n + 1)
                if n >= 4:
                    dve.wait_ge(yr_out[n % 4], yr_total(n % 4, n - 3))
                if n:
                    dve.wait_ge(yr_ready, n)
                dve.tensor_copy(YR[:, n % 4, :], PS[0:RB, n % 4, :]).then_inc(yr_ready, 1)

        @block.tensor
        def _(pe):
            use = [0, 0]
            ident = lambda n: IDN[0:n, 0:n]

            def tile_rows(a, slot, c0, ks, k0, xhi, xlo, first, last, ready=None):
                for n, k in enumerate(ks):
                    if ready is not None:
                        pe.wait_ge(ready[0], ready[1] + k + 1)
                    for w, xs in ((WHI, (xhi, xlo)), (WLO, (xhi,))):
                        for half in range(2):
                            for x in xs:
                                ins = pe.matmul(acc[a][:, half, 0:HALF], w[:, slot, k, c0:c0 + P], x[:, k0 + k, HALF * half:HALF * half + HALF],
                                                start=first and n == 0 and w is WHI and x is xhi, stop=last and n == len(ks) - 1 and w is WLO)
                return ins

            pe.wait_ge(in_consts, 16)
            pe.wait_ge(in_vecs, 96)
            pe.transpose(PS[:, 4, 0:50], VEC[0:50, :], ident(50)).then_inc(vec_tr, 1)
            pe.wait_ge(in_x, 112)
            for g in range(10):
                i, c4 = g // 2, g % 2
                if g >= 4:
                    pe.wait_ge(xe_a if g % 2 else xe_d, (g - 4) // 2 + 1)
                for c in range(4):
                    ins = pe.transpose(PS[:, g % 4, RB * c:RB * c + RB], XROW[:, i, P * (4 * c4 + c):P * (4 * c4 + c) + P], ident(RB))
                ins.then_inc(x_tr, 1)

            def norm(name):
                n = norm_no[name]
                if n:
                    pe.wait_ge(rt_ready, n)
                for c in range(KC):
                    pe.wait_ge(sq_ready, KC * n + c + 1)
                    for half in range(2):
                        ins = pe.matmul(PS[:, 6 + half, 0:HALF], ONE, SQ[:, c % 2, HALF * half:HALF * half + HALF], start=c == 0, stop=c == KC - 1)
                    ins.then_inc(sq_used, 1)

            def take(a):
                if use[a]:
                    pe.wait_ge(acc_free[a], use[a])
                use[a] += 1

            def even_slab(s):
                pe.wait_ge(lo_done, s + 1)
                for j in range(EVEN_TILES[s]):
                    take(j)
                    ins = tile_rows(j, s % 2, P * j, range(KC), 0, HHI, HLO, True, True, (h_ready, 0) if s == 0 and j == 0 else None)
                    ins.then_inc(acc_done if j + 1 < EVEN_TILES[s] else slab_used, 1)

            norm("mix0")
            for s in range(4):
                even_slab(s)

            pe.wait_ge(acc_free[0], 4)
            for i in range(NRB):
                m = blk(i)[0]
                pe.transpose(PS[0:m, 4, 8 * i:8 * i + 8], WIT[0:8, RB * i:RB * i + m], ident(8))
            pe.matmul(PS[:, 5, 0:NS], CA[0:8, C_A8:C_A8 + P], WIT[0:8, LP:R], start=True, stop=True).then_inc(wi_tr, 1)
            pe.wait_ge(acc_free[1], 2)

            pe.wait_ge(wsel_ready, 2)
            pe.wait_ge(rt_ready, 1)
            for i in range(1, NRB):
                m, nk = blk(i)
                for h in range(IH):
                    n = IH * (i - 1) + h
                    if n >= 2:
                        pe.wait_ge(relu_done, n - 1)
                    lo = 64 * (h % 2)
                    for half in range(2):
                        ins = pe.matmul(PS[0:m, 4 + 2 * (n % 2) + half, 0:nk // 2], QIT[lo:lo + 64, h // 2, RB * i:RB * i + m],
                                        KID[lo:lo + 64, half * (nk // 2):(half + 1) * (nk // 2)], start=True, stop=True)
                    ins.then_inc(il_ready, 1)

            def kit(n):
                pe.wait_ge(kidx_in[n % 4], 16 * (n // 4 + 1))
                for u in range(2):
                    if n:
                        pe.wait_ge(kit_ready, 2 * (n - 1) + u + 1)
                    for j in range(4):
                        ins = pe.transpose(PS[:, 4 + u, P * j:P * j + P], KI[:, n % 4, 8 * u + 2 * j:8 * u + 2 * j + 2, :].rearrange("p a d -> p (a d)"), ident(P))
                    ins.then_inc(kit_tr, 1)

            pe.wait_ge(relu_done, 4 * IH)
            pe.wait_ge(qis_ready, 4)
            pe.wait_ge(acc_free[1], 3)
            kit(0)
            for gi, g in enumerate((1, 0)):
                for b4 in range(4):
                    n, b = 4 * gi + b4, 4 * g + b4
                    if n + 1 < DB:
                        kit(n + 1)
                    pe.wait_ge(kit_ready, 2 * n + 2)
                    if n == 4:
                        pe.wait_ge(sr_done, 5)
                    for u in range(2):
                        for hf in range(2):
                            pe.matmul(PS[32 * b4:32 * b4 + 32, 2 * u + hf, :], QIS[64 * hf:64 * hf + 64, b, :, :].rearrange("p h t -> p (h t)"),
                                      KIT[64 * hf:64 * hf + 64, n % 2, 512 * u:512 * u + 512], start=True, stop=True)
                    pe.matmul(PS[32 * b4:32 * b4 + 32, 6, 0:NS], QIS[0:64, b, :, :].rearrange("p h t -> p (h t)"), KID[0:64, LP:R],
                              start=True, stop=True).then_inc(ss_done, 1)
                pe.wait_ge(sr_done, 5 * gi + 5)
                for q in range(5):
                    w = 512 if q < 4 else NS
                    if 5 * gi + q:
                        pe.wait_ge(comb_evac, 5 * gi + q)
                    pe.matmul(PS[0:NS, 7, 0:w], WSEL[:, g, :], SR[:, 512 * q:512 * q + w], start=True, stop=True).then_inc(comb_done, 1)

            for s in range(4, 8):
                even_slab(s)

            pe.wait_ge(in_spn, 16)
            for g in range(4):
                ins = pe.transpose(PS[:, 6, 120 * g:120 * g + 120], SPN[:, P * g:P * g + P], ident(120))
            ins.then_inc(sp_tr, 1)
            for i in range(6):
                m = RB if i < 4 else (LAST if i == 4 else NS)
                r0 = RB * i if i < 5 else LP
                if i >= 2:
                    pe.wait_ge(kvr_ready, i - 1)
                pe.transpose(PS[0:m, 4 + i % 2, 0:P], KT[:, r0:r0 + m], ident(P))
                pe.transpose(PS[0:m, 4 + i % 2, P:2 * P], VT[:, r0:r0 + m], ident(P))
                pe.transpose(PS[0:m, 4 + i % 2, 2 * P:2 * P + HD], KID[0:64, r0:r0 + m], ident(64)).then_inc(kvr_tr, 1)
            pe.wait_ge(acc_free[0], 8)
            pe.wait_ge(acc_free[1], 7)
            pe.wait_ge(sp_ready, 1)
            for g in range(4):
                ins = pe.transpose(PS[0:PB, 6, P * g:P * g + P], UE[:, g, EXT - PB:EXT], ident(P))
            ins.then_inc(uo_tr, 1)
            for g in range(4):
                ins = pe.transpose(PS[0:NS, 7, P * g:P * g + P], UN[:, g, :], ident(P))
            ins.then_inc(uo_tr, 1)

            pe.wait_ge(uo_ready, 2)
            pe.wait_ge(kvr_ready, 6)
            pe.wait_ge(casts, 1)
            pe.wait_ge(in_pw, 16)

            def logits(n):
                i, h = divmod(n, NH)
                m, nk = blk(i)
                kv, lo = h // GRP, 64 * (h % 2)
                if n >= 2:
                    pe.wait_ge(exp_done, n - 1)
                if h == 0:
                    pe.wait_ge(nm_final, i + 1)
                keys = KT if kv == h % 2 else KX
                for half in range(2):
                    ks = slice(half * (nk // 2), (half + 1) * (nk // 2))
                    pe.matmul(PS[0:m, 4 + 2 * (n % 2) + half, 0:nk // 2], QT[lo:lo + 64, h // 2, RB * i:RB * i + m], keys[lo:lo + 64, ks], start=True, stop=False)
                    ins = pe.matmul(PS[0:m, 4 + 2 * (n % 2) + half, 0:nk // 2], IDB[0:m, 0:m], NM[0:m, i, ks], start=False, stop=True)
                ins.then_inc(lg_ready, 1)

            def flip(n):
                i, h = divmod(n, NH)
                m, nk = blk(i)
                pe.wait_ge(pr_ready, n + 1)
                if n:
                    pe.wait_ge(pt_evac, n)
                if n and n % NH == 0:
                    pe.wait_ge(ylo, n // NH)
                for j in range(i + 1):
                    kb = blk(j)[0]
                    out = PS[0:kb, 0, RB * j:RB * j + m] if j < 4 else PS[0:kb, 1, 0:m]
                    ins = pe.transpose(out, PR[0:m, n % 2, RB * j:RB * j + kb], ident(m))
                ins.then_inc(pt_tr, 1)

            def values(n):
                i, h = divmod(n, NH)
                m, nk = blk(i)
                kv, lo, pair = h // GRP, 64 * (h % 2), n // 2
                pe.wait_ge(pt_evac, n + 1)
                if n % 2 == 0 and pair >= 2:
                    pe.wait_ge(olo, pair - 1)
                for j in range(i + 1):
                    kb = blk(j)[0]
                    ins = pe.matmul(PS[lo:lo + 64, 2 + pair % 2, 0:m], KVR[0:kb, j, P + 64 * kv:P + 64 * kv + 64], PT[0:kb, n % 2, j, 0:m], start=j == 0, stop=j == i)
                ins.then_inc(pv_done, 1)

            NST = NRB * NH
            logits(0)
            for n in range(NST):
                if n + 1 < NST:
                    logits(n + 1)
                flip(n)
                if n:
                    values(n - 1)
                if n % NH == NH - 1 and n // NH < 4:
                    g = n // NH
                    pe.wait_ge(pd_ready, g + 1)
                    pe.wait_ge(pt_evac, n + 1)
                    for half in range(2):
                        ins = pe.matmul(PS[:, half, 0:HALF], PW[:, g, :], PD[:, HALF * half:HALF * half + HALF], start=True, stop=True)
                    ins.then_inc(y_done, 1)
            values(NST - 1)

            pe.wait_ge(exp_done, NST)
            pe.wait_ge(olo, NST // 2)
            pe.wait_ge(nms_ready, 1)
            pe.wait_ge(qbd_ready, 9)
            for g in range(2):
                for b4 in range(4):
                    nb = 4 * g + b4
                    q = 8 * g + b4
                    pe.wait_ge(kv_in[q % 2], 16 * (q // 2 + 1))
                    for u in range(4):
                        if g and b4 == 0 and u < 2:
                            pe.wait_ge(*((spt_evac, 3) if u == 0 else (spt_evac2, 2)))
                        if 2 * nb + u // 2:
                            pe.wait_ge(kts_evac2 if u % 2 else kts_evac, 2 * nb + u // 2)
                        for j in range(4):
                            ins = pe.transpose(PS[:, 6 + u % 2, P * j:P * j + P], KN[:, q % 2, 4 * u + j, :], ident(P))
                        ins.then_inc(kts_tr, 1)
                    pe.wait_ge(kts_evac, 2 * nb + 2)
                    pe.wait_ge(kts_evac2, 2 * nb + 2)
                    if g and b4 == 0:
                        pe.wait_ge(sexp, 1)
                    lhs = QBD[:, nb, :, :].rearrange("p k n -> p (k n)")
                    for c in range(4):
                        pe.matmul(PS[32 * b4:32 * b4 + 32, c, :], lhs, KTS[:, 512 * c:512 * c + 512], start=True, stop=False)
                    pe.matmul(PS[32 * b4:32 * b4 + 32, 4, 0:NS], lhs, KT[:, LP:R], start=True, stop=False).then_inc(slg, 1)
                for c in range(5):
                    w = 512 if c < 4 else NS
                    mask = NMS[:, 0:PAST].rearrange("p (s t) -> p t s", t=TOK)[:, 4 * c:4 * c + 4, :] if c < 4 else NMS[:, PAST:SKEYS]
                    ins = pe.matmul(PS[:, c, 0:w], EXB[:, g, :], mask, start=False, stop=True)
                ins.then_inc(slg_mask, 1)
                pe.wait_ge(sp_norm, g + 1)
                for u in range(5):
                    if u in (2, 4):
                        pe.wait_ge(spt_evac, 3 * g + u // 2)
                    if u == 3:
                        pe.wait_ge(spt_evac2, 2 * g + 1)
                    if u < 4:
                        for j in range(4):
                            ins = pe.transpose(PS[:, 6 + u % 2, P * j:P * j + P], SR[:, P * (4 * u + j):P * (4 * u + j) + P], ident(P))
                    else:
                        ins = pe.transpose(PS[0:NS, 6, 0:P], SR[:, PAST:SKEYS], ident(P))
                    ins.then_inc(spt_tr, 1)
                pe.wait_ge(spt_evac, 3 * g + 3)
                pe.wait_ge(spt_evac2, 2 * g + 2)
                if g:
                    pe.wait_ge(solo, 8)
                for b4 in range(4):
                    q = 8 * g + 4 + b4
                    pe.wait_ge(kv_in[q % 2], 16 * (q // 2 + 1))
                    for pg in range(TOK):
                        pe.matmul(PS[:, 5, 32 * b4:32 * b4 + 32], KN[:, q % 2, pg, :], PTS[:, pg, 32 * b4:32 * b4 + 32], start=pg == 0, stop=False)
                    pe.matmul(PS[:, 5, 32 * b4:32 * b4 + 32], KVR[0:NS, 5, P:2 * P], PTS[0:NS, TOK, 32 * b4:32 * b4 + 32], start=False, stop=True).then_inc(spv, 1)

            def slab_loop(g, xhi, xlo, ready=None):
                with pe.Fori(0, g.iters) as i:
                    for q in range(2):
                        pe.wait_ge(lo_done, g.slab0 + 2 * i + q + 1)
                        for j in range(2):
                            pe.wait_ge(acc_free[j], (g.use0, g.use1)[j] + 2 * i + q)
                            tile_rows(j, (g.slab0 + q) % 2, P * j, range(KC), 0, xhi, xlo, True, True, ready if q == 0 and j == 0 else None).then_inc(slab_used if j else acc_done, 1)

            def down_loop(g):
                kc = g.kcs[0]
                with pe.Fori(0, g.iters) as i:
                    for q in range(2):
                        pe.wait_ge(lo_done, g.slab0 + 2 * i + q + 1)
                        for j in range(2):
                            if q == 0:
                                pe.wait_ge(acc_free[j], (g.use0, g.use1)[j] + i)
                            ins = tile_rows(j, (g.slab0 + q) % 2, P * j, range(kc), kc * q, AHI, ALO, q == 0, q == 1)
                            if j:
                                ins.then_inc(slab_used, 1)
                            elif q:
                                ins.then_inc(acc_done, 1)

            pe.wait_ge(sohi, 16)
            pe.wait_ge(solo, 16)
            pe.wait_ge(ylo, 4)
            slab_loop(gemms["out0"], HHI, HLO)

            def ffn(l):
                norm(f"ffn{l}")
                n = norm_no[f"ffn{l}"]
                for half in "ab":
                    g = gemms[f"up{l}{half}"]
                    slab_loop(g, HHI, HLO, (h_ready, KC * n) if half == "a" else None)
                    pe.wait_ge(alo_ready, a0[g] + 2 * g.iters + 1)
                    down_loop(gemms[f"down{l}{half}"])

            ffn(0)
            norm("mix1")
            g = gemms["gd"]
            pe.wait_ge(lo_done, g.slab0 + 1)
            pe.wait_ge(acc_free[0], g.use0)
            tile_rows(0, g.slab0 % 2, 0, range(KC), 0, HHI, HLO, True, True, (h_ready, KC * norm_no["mix1"])).then_inc(slab_used, 1)
            slab_loop(gemms["oq"], HHI, HLO)
            pe.wait_ge(acc_free[0], g.use0 + 1)
            pe.wait_ge(in_wgu, 16)
            pe.wait_ge(rt_ready, norm_no["mix1"] + 1)
            for h in range(GH):
                if h >= 2:
                    pe.wait_ge(la_min, h - 1)
                for half in range(2):
                    ins = pe.matmul(PS[:, 4 + 2 * (h % 2) + half, 0:HALF], WGU[:, GDK * h:GDK * h + GDK], GD[:, HALF * half:HALF * half + HALF], start=True, stop=True)
                ins.then_inc(la_mm, 1)
            slab_loop(gemms["okv"], HHI, HLO)
            g = gemms["okv"]
            pe.wait_ge(acc_free[0], g.use0 + 2 * g.iters)
            pe.wait_ge(acc_free[1], g.use1 + 2 * g.iters)
            pe.wait_ge(la_min, GH)
            pe.wait_ge(pads0, 1)

            for v in range(14):
                hp, n = divmod(v, 7)
                if n < 6:
                    u = 6 * hp + n
                    pe.wait_ge(lev_q, u + 1)
                    pe.wait_ge(lev_k, u + 1)
                    qs, ks = LQ[:, u % 2], LK[:, u % 2]
                else:
                    qs, ks = G[:, 2 * hp:2 * hp + 2, :], G[:, 4 + 2 * hp:6 + 2 * hp, :]
                if v >= 2:
                    pe.wait_ge(att_ev, v - 1)
                bank = 4 + 2 * (v % 2)
                for par in range(2):
                    for c in range(NCP if n < 4 else NCH):
                        m = CH if c < NCP else NS
                        ps = PS[64 * par:64 * par + m, bank + c // 8, CH * (c % 8):CH * (c % 8) + m]
                        ins = pe.matmul(ps, ks[:, par, CH * c:CH * c + m], qs[:, par, CH * c:CH * c + m], start=True, stop=True)
                ins.then_inc(att_done, 1)

            def chunk_rows(c):
                m = CH if c < NCP else NS
                if c:
                    pe.wait_ge(vk_ev, c)
                for h in range(GH):
                    for e in range(2):
                        pe.transpose(PS[0:m, h % 2, 256 * (h // 2) + 128 * e:256 * (h // 2) + 128 * e + 128], G[:, 8 + 2 * h + e, CH * c:CH * c + m], ident(P))
                for h in range(GH):
                    x = 256 * (h % 2) + 128 * (h // 2)
                    ins = pe.transpose(PS[0:m, 2, x:x + 128], G[:, 4 + h, CH * c:CH * c + m], ident(P))
                ins.then_inc(vk_tr, 1)

            def chunk_products(c):
                m = CH if c < NCP else NS
                if c:
                    pe.wait_ge(o_ev, c)
                if 0 < c < NCP:
                    pe.wait_ge(s_new, GH * c)
                for h in range(GH):
                    rows = slice(64 * (h % 2), 64 * (h % 2) + m)
                    for e in range(2):
                        out = PS[:, 3 + h % 2, m * (2 * (h // 2) + e):m * (2 * (h // 2) + e) + m]
                        inter = 0 < c < NCP
                        if inter:
                            pe.matmul(out, STATE[:, c % 2, h, 128 * e:128 * e + 128], G[:, h, CH * c:CH * c + m], start=True, stop=False)
                        x = GDV * (h // 2) + 128 * e
                        ins = pe.matmul(out, VR[rows, c % 2, x:x + 128], ATT[rows, h // 2, CH * c:CH * c + m], start=not inter, stop=True)
                ins.then_inc(o_done, 1)

            pe.wait_ge(kh_ready, 2)
            pe.wait_ge(qe_ready, 2)
            pe.wait_ge(att_ev, 14)
            chunk_rows(0)
            for c in range(NCP):
                pe.wait_ge(vk_ev, c + 1)
                if c:
                    pe.wait_ge(s_new, GH * c)
                for h in range(GH):
                    rows = slice(64 * (h % 2), 64 * (h % 2) + CH)
                    x = h // 2
                    ins = pe.matmul(PS[:, 5 + h % 2, GDV * (h // 2):GDV * (h // 2) + GDV], KR[rows, c % 2, GDK * x:GDK * x + GDK], VR[rows, c % 2, GDV * x:GDV * x + GDV], start=True, stop=True)
                ins.then_inc(u_done, 1)
                chunk_rows(c + 1)
                chunk_products(c)
            pe.wait_ge(vk_ev, NCH)
            chunk_products(NCP)
            pe.wait_ge(s_new, GH * NCP)
            for b in range(DB):
                pe.wait_ge(st_in[b % 2], 16 * (b // 2 + 1))
                pe.wait_ge(kb_ready, b + 1)
                if b >= 2:
                    pe.wait_ge(sn_ready, GH * (b - 1))
                bank = 5 if b % 2 else 0
                for h in range(GH):
                    rows, x = slice(64 * (h % 2), 64 * (h % 2) + NS), h // 2
                    ins = pe.matmul(PS[:, bank + h % 2, GDV * (h // 2):GDV * (h // 2) + GDV], KB[rows, b % 2, GDK * x:GDK * x + GDK], VR[rows, NCP % 2, GDV * x:GDV * x + GDV], start=True, stop=True)
                ins.then_inc(su_done, 1)
                for h in range(GH):
                    for e in range(2):
                        y = NS * (2 * h + e) + DT * b
                        ins = pe.matmul(PS[:, 7, y:y + DT], SIN[:, b % 2, h, 128 * e:128 * e + 128], G[:, h, WP + DT * b:WP + DT * b + DT], start=True, stop=True)
                ins.then_inc(oi_done, 1)
            pe.wait_ge(in_cg, 16)
            pe.wait_ge(sn_ready, GH * DB)
            for h in range(GH):
                if h >= 2:
                    pe.wait_ge(ort, h - 1)
                for e in range(2):
                    n = 2 * h + e
                    pe.wait_ge(osq_ready, n + 1)
                    for half in range(2):
                        ins = pe.matmul(PS[:, 4 + 2 * (h % 2) + half, 0:HALF], CG[:, G_ONE:G_ONE + P], GSC[:, n % 2, HALF * half:HALF * half + HALF], start=e == 0, stop=e == 1)
                    ins.then_inc(osq_used, 1)
            slab_loop(gemms["og"], HHI, HLO)
            pe.wait_ge(o2lo, KC)
            slab_loop(gemms["out1"], HHI, HLO)
            ffn(1)
            norm("final")
            n0 = KC * norm_no["final"]
            for n in range(2 * NRB):
                c4, i = divmod(n, NRB)
                pe.wait_ge(ht_ready, n0 + 4 * c4 + 4)
                if n >= 4:
                    pe.wait_ge(yr_ready, n - 3)
                for c in range(4):
                    ins = pe.transpose(PS[0:RB, n % 4, P * c:P * c + P], XT[:, 4 * c4 + c, RB * i:RB * i + RB], ident(P))
                ins.then_inc(y_tr, 1)


INS = ["x_prompt", "x_sample", "cache_k", "cache_v", "cache_kidx", "state_pool", "state_gla", "page_table", "meta_tokens",
       "norm_mix", "norm_ffn", "norm_final", "w_in_even", "w_out_even", "pool_w", "pool_scale", "w_in_odd", "gla_w_gate_up",
       "gla_b_gate", "gla_norm", "w_out_odd", "ffn_w_gate", "ffn_w_up", "ffn_w_down"]
OUTS = [("y_prompt", (1, SEQ, D)), ("y_sample", (DB, DT, D)),
        ("new_k_prompt", (1, 1, LP, NKV, HD)), ("new_v_prompt", (1, 1, LP, NKV, HD)), ("new_kidx_prompt", (1, 1, LP, HD)),
        ("new_k_sample", (1, DB, DT, NKV, HD)), ("new_v_sample", (1, DB, DT, NKV, HD)), ("new_kidx_sample", (1, DB, DT, HD)),
        ("new_pool_prompt", (1, 1, PB, 512)), ("new_pool_sample", (1, DB, PB, 512)),
        ("new_gla_prompt", (1, 1, GH, GDK, GDV)), ("new_gla_sample", (1, DB, GH, GDK, GDV))]


def shape_constants():
    import numpy as np

    a = np.zeros((P, C_A), np.float32)
    a[:, C_ID:C_ID + P] = np.eye(P)
    a[:, C_ONE:C_ONE + P] = 1.0 / D
    p = np.arange(P)
    b4, h, tt = p // 32, p % 32 // 4, p % 4
    a[0:8, C_A8:C_A8 + P] = np.arange(8)[:, None] == h[None, :]
    col = np.arange(NS)
    for g in range(2):
        a[:, C_DM + NS * g:C_DM + NS * g + NS] = (col[None, :] // DT == 4 * g + b4[:, None]) & (col[None, :] % DT == tt[:, None])
        a[0:NS, C_EX + P * g:C_EX + P * g + P] = a[:, C_DM + NS * g:C_DM + NS * g + NS].T
    seen = (col[None, :] // DT == col[:, None] // DT) & (col[None, :] % DT <= col[:, None] % DT)
    a[0:NS, C_VN:C_VN + NS] = seen
    a[0:NS, C_FN:C_FN + NS] = np.where(seen, 0.0, HIDDEN)
    for g in range(4):
        w = 2 << g
        a[:, C_INV + 16 * g:C_INV + 16 * g + 16] = 1.0 / np.minimum(w, np.arange(16) + 1.0)
    a[:, C_EPS] = EPS
    a[:, C_SUB] = np.arange(P) % SUB
    c = np.zeros((P, C_G), np.float32)
    c[:, G_ONE:G_ONE + P] = 1.0 / GDV
    s, q = np.arange(CH)[:, None], np.arange(CH)[None, :]
    for n, size in enumerate(LEVELS):
        same = s // size == q // size
        c[0:CH, G_MASK + CH * n:G_MASK + CH * n + CH] = same & (s % size < size // 2) & (q % size >= size // 2)
    c[0:CH, G_MASK + CH * 6:G_MASK + CH * 7] = s == q
    rst = np.ones(GWP)
    rst[0:LEAD + LP:CH] = 0
    rst[LEAD + LP::DT] = 0
    c[:, G_RST:G_RST + GWP] = rst
    c[0:NS, G_SB:G_SB + DB] = np.arange(NS)[:, None] // DT == np.arange(DB)[None, :]
    c[CH:P, G_MASK:G_MASK + 7 * CH] = c[0:CH, G_MASK:G_MASK + 7 * CH]
    c[CH:P, G_SB:G_SB + DB] = c[0:CH, G_SB:G_SB + DB]
    return a, c


def kernel(**inputs):
    import concourse.bacc as bacc
    import numpy as np
    from concourse.bass_utils import run_bass_kernel_spmd

    nc = bacc.Bacc("TRN2", target_bir_lowering=False, num_devices=1, dynamic_dma_scratch_size=1024)
    arrays = {"in_" + name: np.ascontiguousarray(inputs[name]) for name in INS}
    arrays["in_page_table"] = np.ascontiguousarray(inputs["page_table"].T)
    for name, a in zip(("consts_a", "consts_g"), shape_constants()):
        arrays["in_" + name] = a
    ins = {name[3:]: nc.dram_tensor(name, a.shape, mybir.dt.from_np(a.dtype), kind="ExternalInput").ap() for name, a in arrays.items()}
    outs = {name: nc.dram_tensor("out_" + name, shape, F32, kind="ExternalOutput").ap() for name, shape in OUTS}
    trunk(nc, ins, outs)
    r = run_bass_kernel_spmd(nc, [arrays], core_ids=[0])
    return tuple(r.results[0]["out_" + name] for name, _ in OUTS)
```
